# Optimizing a Trainium2 kernel written in Bass

```python
import math
import jax, jax.numpy as jnp
from jax import lax
import numpy as np

D_MODEL = 1024
BATCH = 1
SEQ = 512
DEPTH = 2

EPS = 1e-6
A_WIDTH = 256
A_GROUPS = 4
A_GROUP_DIM = A_WIDTH // A_GROUPS
A_CHUNK = 128
MLA_HEADS = 8
Q_LORA = 384
KV_LORA = 256
QK_NOPE = 64
QK_ROPE = 32
V_DIM = 64
QK_DIM = QK_NOPE + QK_ROPE
ROPE_THETA = 10000.0
Q_BLOCK = 128
POOL_WINDOWS = (2, 4, 8, 16)
C_WIDTH = 256
C_GROUP = C_WIDTH // len(POOL_WINDOWS)
N_BRANCH = 3
SPLITS = (A_WIDTH, 2 * A_WIDTH, 2 * A_WIDTH + Q_LORA, 2 * A_WIDTH + Q_LORA + KV_LORA,
          2 * A_WIDTH + Q_LORA + KV_LORA + QK_ROPE,
          2 * A_WIDTH + Q_LORA + KV_LORA + QK_ROPE + C_WIDTH)
IN_COLS = SPLITS[-1] + N_BRANCH * D_MODEL
PEER_HEADS = 8
N_KEYS = 128
N_EXPERTS = N_KEYS * N_KEYS
PEER_DKEY = 256
PEER_HALF = PEER_DKEY // 2
PEER_TOPK = 16
PEER_BLOCK = 128

kernel_name = "hybrid_gated_mixers_peer_trunk"

def _rmsnorm(x, gain=None):
    xf = x.astype(jnp.float32)
    y = xf * lax.rsqrt(jnp.mean(xf * xf, axis=-1, keepdims=True) + EPS)
    if gain is not None:
        y = y * gain.astype(jnp.float32)
    return y.astype(x.dtype)

def _layernorm(x):
    xf = x.astype(jnp.float32)
    mu = jnp.mean(xf, axis=-1, keepdims=True)
    d = xf - mu
    return (d * lax.rsqrt(jnp.mean(d * d, axis=-1, keepdims=True) + EPS)).astype(x.dtype)

def _modulate(h, shift, scale):
    return h * (1 + scale[:, None, :]) + shift[:, None, :]

def _rope(x, cos, sin):
    half = x.shape[-1] // 2
    x1, x2 = x[..., :half], x[..., half:]
    cos = cos.astype(x.dtype)
    sin = sin.astype(x.dtype)
    return jnp.concatenate([x1 * cos - x2 * sin, x2 * cos + x1 * sin], axis=-1)

def _spatial_gating(u, v, w_s, b_s):
    B, S, _ = u.shape
    vn = _layernorm(v).reshape(B, S // A_CHUNK, A_CHUNK, A_GROUPS, A_GROUP_DIM)
    mixed = jnp.einsum('gts,bnsgc->bntgc', jnp.tril(w_s).astype(vn.dtype), vn)
    mixed = mixed + b_s.T.astype(vn.dtype)[:, :, None]
    return u * mixed.reshape(B, S, A_WIDTH)

def _mla(cq, ckv, kr, q_norm, w_uq, kv_norm, w_ukv, cos, sin):
    B, S, _ = cq.shape
    q = (_rmsnorm(cq, q_norm) @ w_uq).reshape(B, S, MLA_HEADS, QK_DIM)
    q = jnp.concatenate([q[..., :QK_NOPE], _rope(q[..., QK_NOPE:], cos, sin)], axis=-1)
    kv = (_rmsnorm(ckv, kv_norm) @ w_ukv).reshape(B, S, MLA_HEADS, QK_NOPE + V_DIM)
    k_rope = _rope(kr[:, :, None, :], cos, sin)
    k = jnp.concatenate([kv[..., :QK_NOPE],
                         jnp.broadcast_to(k_rope, (B, S, MLA_HEADS, QK_ROPE))], axis=-1)
    v = kv[..., QK_NOPE:]
    q = q.transpose(0, 2, 1, 3) * (1.0 / math.sqrt(QK_DIM))
    k = k.transpose(0, 2, 1, 3)
    v = v.transpose(0, 2, 1, 3)
    nq = S // Q_BLOCK
    qb = q.reshape(B, MLA_HEADS, nq, Q_BLOCK, QK_DIM).transpose(2, 0, 1, 3, 4)
    key_pos = jnp.arange(S)

    def block(args):
        qi, bi = args
        s = jnp.einsum('bhqd,bhkd->bhqk', qi, k).astype(jnp.float32)
        q_pos = bi * Q_BLOCK + jnp.arange(Q_BLOCK)
        s = jnp.where(key_pos[None, :] <= q_pos[:, None], s, -jnp.inf)
        p = jax.nn.softmax(s, axis=-1)
        return jnp.einsum('bhqk,bhkd->bhqd', p.astype(v.dtype), v)

    o = lax.map(block, (qb, jnp.arange(nq)))
    o = o.transpose(1, 0, 3, 2, 4).reshape(B, S, MLA_HEADS * V_DIM)
    return o

def _multiscale_pool(z, w_pool, pool_scale):
    B, S, _ = z.shape
    zf = z.astype(jnp.float32)
    t = jnp.arange(S)
    outs = []
    for gi, w in enumerate(POOL_WINDOWS):
        zg = zf[..., gi * C_GROUP:(gi + 1) * C_GROUP]
        cs = jnp.cumsum(jnp.pad(zg, ((0, 0), (w, 0), (0, 0))), axis=1)
        win = cs[:, w:] - cs[:, :S]
        cnt = jnp.minimum(t + 1, w).astype(jnp.float32)[None, :, None]
        outs.append((win / cnt - zg) @ w_pool[gi].astype(jnp.float32))
    y = jnp.concatenate(outs, axis=-1) * pool_scale.astype(jnp.float32)
    return y.astype(z.dtype)

def _peer(h, w_pq, sub_keys, u_tab, v_tab):
    B, S, D = h.shape
    T = B * S
    xb = h.reshape(T // PEER_BLOCK, PEER_BLOCK, D)

    def block(xt):
        q = (xt @ w_pq).reshape(PEER_BLOCK, PEER_HEADS, 2, PEER_HALF)
        s = jnp.einsum('thpd,hpkd->thpk', q, sub_keys)
        v1, i1 = lax.top_k(s[:, :, 0], PEER_TOPK)
        v2, i2 = lax.top_k(s[:, :, 1], PEER_TOPK)
        cand = (v1[..., :, None] + v2[..., None, :]).reshape(PEER_BLOCK, PEER_HEADS, -1)
        cidx = (i1[..., :, None] * N_KEYS + i2[..., None, :]).reshape(PEER_BLOCK, PEER_HEADS, -1)
        top, pos = lax.top_k(cand, PEER_TOPK)
        eidx = jnp.take_along_axis(cidx, pos, axis=-1)
        g = jax.nn.softmax(top.astype(jnp.float32), axis=-1).astype(xt.dtype)
        ue = u_tab[eidx]
        a = jax.nn.gelu(jnp.einsum('thkd,td->thk', ue, xt))
        ve = v_tab[eidx]
        return jnp.einsum('thk,thkd->td', g * a, ve)

    return lax.map(block, xb).reshape(B, S, D)

def setup_inputs(seed: int = 0) -> dict:
    key = jax.random.key(seed)
    ks = jax.random.split(key, 24)
    f32 = jnp.float32
    nrm = lambda k, shape, s: jax.random.normal(k, shape, f32) * s
    L, D = DEPTH, D_MODEL
    x = nrm(ks[0], (BATCH, SEQ, D), 1.0)
    c = nrm(ks[1], (BATCH, D), 1.0)
    offs = jax.random.randint(ks[2], (BATCH, 1), 0, 4096, dtype=jnp.int32)
    positions = (offs + jnp.arange(SEQ, dtype=jnp.int32)[None, :]).astype(jnp.int32)
    return {
        "x": x,
        "c": c,
        "positions": positions,
        "w_mod": nrm(ks[3], (L, D, 6 * D), 0.5 * D ** -0.5),
        "b_mod": nrm(ks[4], (L, 6 * D), 0.02),
        "w_in": nrm(ks[5], (L, D, IN_COLS), D ** -0.5),
        "w_s": nrm(ks[6], (L, A_GROUPS, A_CHUNK, A_CHUNK), A_CHUNK ** -0.5),
        "b_s": 1.0 + nrm(ks[7], (L, A_GROUPS, A_CHUNK), 0.02),
        "q_norm": 1.0 + nrm(ks[8], (L, Q_LORA), 0.02),
        "w_uq": nrm(ks[9], (L, Q_LORA, MLA_HEADS * QK_DIM), Q_LORA ** -0.5),
        "kv_norm": 1.0 + nrm(ks[10], (L, KV_LORA), 0.02),
        "w_ukv": nrm(ks[11], (L, KV_LORA, MLA_HEADS * (QK_NOPE + V_DIM)), KV_LORA ** -0.5),
        "w_pool": nrm(ks[12], (L, len(POOL_WINDOWS), C_GROUP, C_GROUP), C_GROUP ** -0.5),
        "pool_scale": 1.0 + nrm(ks[13], (L, C_WIDTH), 0.02),
        "w_a": nrm(ks[14], (L, A_WIDTH, D), A_WIDTH ** -0.5),
        "w_b": nrm(ks[15], (L, MLA_HEADS * V_DIM, D), (MLA_HEADS * V_DIM) ** -0.5),
        "w_c": nrm(ks[16], (L, C_WIDTH, D), C_WIDTH ** -0.5),
        "w_o": nrm(ks[17], (L, D, D), D ** -0.5),
        "w_pq": nrm(ks[18], (L, D, PEER_HEADS * PEER_DKEY), D ** -0.5),
        "sub_keys": nrm(ks[19], (L, PEER_HEADS, 2, N_KEYS, PEER_HALF), PEER_HALF ** -0.5),
        "u_tab": nrm(ks[20], (L, N_EXPERTS, D), D ** -0.5),
        "v_tab": nrm(ks[21], (L, N_EXPERTS, D), 0.5),
        "final_norm": 1.0 + nrm(ks[22], (D,), 0.02),
    }

def reference(x, c, positions, w_mod, b_mod, w_in, w_s, b_s, q_norm, w_uq, kv_norm, w_ukv,
              w_pool, pool_scale, w_a, w_b, w_c, w_o, w_pq, sub_keys, u_tab, v_tab, final_norm):
    B, S, D = x.shape
    inv_freq = 1.0 / (ROPE_THETA ** (jnp.arange(0, QK_ROPE, 2, dtype=jnp.float32) / QK_ROPE))
    ang = positions.astype(jnp.float32)[..., None] * inv_freq
    cos = jnp.cos(ang)[:, :, None, :]
    sin = jnp.sin(ang)[:, :, None, :]
    c_act = jax.nn.silu(c)
    for l in range(DEPTH):
        mod = c_act @ w_mod[l] + b_mod[l]
        sh1, sc1, g1, sh2, sc2, g2 = jnp.split(mod, 6, axis=-1)
        h = _modulate(_rmsnorm(x), sh1, sc1)
        z = h @ w_in[l]
        zu, zv, cq, ckv, kr, zp, zg = jnp.split(z, SPLITS, axis=-1)
        ya = _spatial_gating(jax.nn.gelu(zu), jax.nn.gelu(zv), w_s[l], b_s[l])
        yb = _mla(cq, ckv, kr, q_norm[l], w_uq[l], kv_norm[l], w_ukv[l], cos, sin)
        yc = _multiscale_pool(zp, w_pool[l], pool_scale[l])
        gates = jax.nn.sigmoid(zg).reshape(B, S, N_BRANCH, D)
        merged = (gates[:, :, 0] * (ya @ w_a[l]) + gates[:, :, 1] * (yb @ w_b[l])
                  + gates[:, :, 2] * (yc @ w_c[l]))
        x = x + g1[:, None, :] * (merged @ w_o[l])
        h2 = _modulate(_rmsnorm(x), sh2, sc2)
        x = x + g2[:, None, :] * _peer(h2, w_pq[l], sub_keys[l], u_tab[l], v_tab[l])
    return _rmsnorm(x, final_norm)


_drawn_inputs = setup_inputs


def setup_inputs(seed=0):
    import zlib

    import numpy as np

    out = dict(_drawn_inputs(seed))
    spreads = {}
    factors = {'b_s': 7.287, 'q_norm': 8.0, 'kv_norm': 8.0, 'pool_scale': 6.129, 'final_norm': 2.831}
    for name, (base, spread) in spreads.items():
        noise = np.random.default_rng([zlib.crc32(name.encode()), seed]).standard_normal(out[name].shape)
        drawn = base * np.exp(spread * noise) if base else spread * noise
        out[name] = __import__('jax').numpy.asarray(drawn.astype(out[name].dtype))
    for name, factor in factors.items():
        out[name] = (out[name] * factor).astype(out[name].dtype)
    return out
```

```python
from concourse import bass, mybir
from concourse.alu_op_type import AluOpType as ALU
import numpy as np

ACT = mybir.ActivationFunctionType
AX = mybir.AxisListType.X
F32 = mybir.dt.float32
F32R = mybir.dt.float32r
I32 = mybir.dt.int32
U32 = mybir.dt.uint32
ds = bass.ds

P = 128
DEPTH = 2
D = 1024
KC = D // P
S = 512
TT = S // P
EPS = 1e-6
HEADS, NOPE, ROPE, VD = 8, 64, 32, 64
QK = NOPE + ROPE
HALF = ROPE // 2
Q_LORA, KV_LORA = 384, 256
WINDOWS = (2, 4, 8, 16)
SCALE = 1.0 / float(np.sqrt(QK))
NEG = -3.0e38
PH, TOPK, NKEYS = 8, 16, 128
TB = 32
NTB = S // TB
AG = 4

N_MOD = 6 * KC
MOD_FIRST = 2 * KC
N_MODX = N_MOD - MOD_FIRST
N_IN = 36
P_KR, P_ZV, P_ZU, P_ZP, P_GATE = 5, 6, 8, 10, 12
T_U = 6
N_T = PH * (2 + T_U)
REST = 8
BLK_U = 4
M_ABC = N_IN
M_WO = M_ABC + KC
M_T = M_WO + KC
M_R1 = M_T + N_T
M_G = M_R1 + REST
M_R2 = M_G + NTB * BLK_U
M_V = M_R2 + REST
M_ALL = M_V + P
A_R1 = PH * T_U
A_G = A_R1 + REST
A_R2 = A_G + NTB * BLK_U
N_BANKED = M_V // 2
RAW, RING = 4, 4
LEAD = 2


def order_of_panels():
    order = []
    for p in range(N_IN):
        order.append(("m", p))
        if p < N_MODX:
            order.append(("mod", MOD_FIRST + p))
    order += [("m", m) for m in range(M_ABC, M_T)]
    return order


ORDER = order_of_panels()
N_HEAD = len(ORDER)
RAW_ALL = N_HEAD + M_ALL - M_T
assert RAW_ALL % RAW == 0 and N_HEAD % RAW == 0 and M_T % RING == 0 and M_ALL % RING == 0
RAW_USES = RAW_ALL // RAW
RAW_OF = {what: n for n, what in enumerate(ORDER)}


def mixer_steps():
    steps = []
    for p in range(8):
        steps.append(("panel", p))
        if 1 <= p <= 5:
            steps.append(("ssq", p - 1))
        if p == 3:
            steps.append(("root", 0))
        if p == 5:
            steps.append(("root", 1))
    for r in range(2 * TT):
        steps.append(("proj", r))
        if r:
            steps.append(("turn", r - 1))
        steps.append(("panel", 8 + r))
    steps.append(("turn", 2 * TT - 1))
    steps.append(("panel", 8 + 2 * TT))
    p = 9 + 2 * TT
    for two in ((("ya", 0), ("ya", 1)), (("ya", 2), ("ya", 3)), (("win", 0), ("win", 1)),
                (("pool", 0), ("pool", 1)), (("win", 2), ("win", 3)), (("pool", 2), ("pool", 3))):
        steps += list(two)
        if p < 22:
            steps.append(("panel", p))
            p += 1
    units = HEADS * TT
    for u in range(units + 2):
        if u < units:
            steps.append(("qk", u))
        if 1 <= u <= units:
            steps.append(("pt", u - 1))
        if u >= 2:
            steps.append(("pv", u - 2))
        if u % 2 == 1 and p < N_IN:
            steps.append(("panel", p))
            p += 1
    assert p == N_IN
    return steps


STEPS = mixer_steps()


class Chain:

    def __init__(self, eng, sem, per_layer):
        self.eng, self.sem, self.per_layer = eng, sem, per_layer
        self.layer, self.base, self.n = 0, 0, 0

    def start(self, layer):
        self.layer, self.base, self.n = layer * self.per_layer, 0, 0

    def mark(self, ins):
        ins.then_inc(self.sem, 1)
        self.n += 1

    def wait(self):
        self.eng.wait_ge(self.sem, self.layer + self.base + self.n)

    def link(self, ins):
        self.mark(ins)
        self.wait()

    def enter(self, i, count):
        self.outer, self.inner, self.count = self.base, self.n, count
        self.base, self.n = i * count + (self.base + self.n), 0

    def leave(self, times):
        assert self.n == self.count, (self.n, self.count)
        self.base, self.n = self.outer, self.inner + times * self.count


DVE_CHAIN = 663


def build_trunk(nc, xT, c, pos, freq, bands, w_mod, b_mod, w_in, w_sT, b_s, qkv_gain, w_uq, w_ukv,
                w_pool, pool_scale, w_abc, w_o, w_pq, keysT, uT_tab, v_tab, fin_gain, out, dve_chain):
    gate_d = nc.dram_tensor("gate_spill", [3 * KC, P, S], F32, kind="Internal").ap()
    h_d = nc.dram_tensor("expert_spill", [P, P, S], F32, kind="Internal").ap()
    g_d = nc.dram_tensor("weight_spill", [P // AG, P, NTB, AG * TB], F32, kind="Internal").ap()

    top_of = [nc.sbuf_base + -nc.sbuf_base % 32]

    def sb(name, shape, dt=F32, at=None):
        size = 4 * int(np.prod(shape[1:]))
        size += -size % 32
        off = top_of[0] if at is None else at
        if at is None:
            top_of[0] += size
        return nc.alloc_sbuf_tensor_at(name, shape, dt, offset=off)

    x_sb = sb("x_sb", [P, KC, S])
    mov = sb("mov", [P, 2, KC, S], F32R)
    raw = sb("raw", [P, RAW, KC, P])
    whl = sb("whl", [P, RING, 2, KC, P], F32R)
    mod = sb("mod_cols", [P, N_MOD])
    bmod = sb("bmod", [P, N_MOD])
    c_act = sb("c_act", [P, D])
    fin = sb("fin", [P, KC])
    ident = sb("ident", [P, P])
    ones = sb("ones", [P, P])
    causal = sb("causal", [P, P])
    zeros = sb("zeros", [P, P], F32R)
    iota = sb("iota", [P, P])
    eps = sb("eps", [P, 1])
    cos = sb("cos", [P, TT, HALF])
    sin = sb("sin", [P, TT, HALF])
    gain = sb("gain", [P, 5])
    pscale = sb("pscale", [P, 2])
    bn6 = sb("bn6", [P, TT, 6])
    bn2 = sb("bn2", [P, TT, 2])
    lnr = sb("lnr", [P, TT])
    mcol = sb("mcol", [P, 1])
    mx = sb("mx", [P, 2])
    nmx = sb("nmx", [P, 2])
    rsum = sb("rsum", [P, 2])
    rinv = sb("rinv", [P, 2])
    sq = sb("sq", [P, 2, S])
    root = sb("root", [P, S])
    free = top_of[0]

    qT = sb("qT", [P, HEADS, S])
    kT = sb("kT", [P, HEADS, S])
    mrg = sb("mrg", [P, 2, KC, S], F32R, at=free)
    vh = sb("vh", [P, TT, HEADS * VD])
    y_at = top_of[0]
    y = sb("y", [P, KC, S])
    ukv = sb("ukv", [P, 2, HEADS * (NOPE + VD)], at=y_at)
    tok = sb("tok", [P, 2, HEADS, QK], at=y_at + 8192)
    lat_at = top_of[0]
    lat = sb("lat", [P, 5, S])
    wsT = sb("wsT", [P, 4, P], at=lat_at)
    bsb = sb("bsb", [P, 4, P], at=lat_at + 2048)
    band = sb("band", [P, 12, P], at=lat_at + 4096)
    gst_at = top_of[0]
    gst = sb("gst", [P, 6, S])
    uq = sb("uq", [P, 3, HEADS * QK], at=gst_at)
    kr = sb("kr", [P, TT, ROPE])
    rt = sb("rt", [P, 4, HEADS, HALF])
    ug = sb("ug", [P, 2, S])
    pv_at = top_of[0]
    vg = sb("vg", [P, TT, 2 * P])
    zp = sb("zp", [P, TT, 2 * P])
    pr = sb("pr", [P, 2, S], at=pv_at)
    prT = sb("prT", [P, 2, S], at=pv_at + 4096)
    wpl = sb("wpl", [P, 2, 64])
    ht_at = top_of[0]
    ytmp = sb("ytmp", [P, 2, S])
    ht = sb("ht", [P, 2, S], at=ht_at)
    assert top_of[0] <= nc.sbuf_usable_end, top_of[0]

    top_of[0] = free
    hst = sb("hst", [P, 2, S])
    topv = sb("topv", [P, TT, PH, TOPK])
    sel1 = sb("sel1", [P, TT, PH, TOPK])
    sel2 = sb("sel2", [P, TT, PH, TOPK])
    den = sb("den", [P, TT * PH])
    dinv = sb("dinv", [P, TT * PH])
    sel1T = sb("sel1T", [P, S])
    sel2T = sb("sel2T", [P, S])
    gT = sb("gT", [P, S])
    gThl = sb("gThl", [P, 2, S], F32R)
    pick_at = top_of[0]
    qh = sb("qh", [P, 2, S])
    keys = sb("keys", [P, 2 * PH, P])
    sc2 = sb("sc2", [P, TT, P])
    v12 = sb("v12", [P, TT, 2, TOPK])
    i12u = sb("i12u", [P, TT, 2, TOPK], U32)
    i12 = sb("i12", [P, TT, 2, TOPK])
    cand = sb("cand", [P, TT, TOPK * TOPK])
    cand2 = sb("cand2", [P, TT, TOPK * TOPK])
    topc = sb("topc", [P, TT, TOPK])
    posu = sb("posu", [P, TT, TOPK], U32)
    abu = sb("abu", [P, 2, TT, TOPK], U32)
    abf = sb("abf", [P, 2, TT, TOPK])
    eq = sb("eq", [P, TT, TOPK, TOPK])
    assert top_of[0] <= nc.sbuf_usable_end
    top_of[0] = pick_at
    stage = sb("stage", [P, 2, P, TB])
    hot2 = sb("hot2", [P, 2, 4, P], F32R)
    hot1 = sb("hot1", [P, 2, 4, P])
    hotg = sb("hotg", [P, 2, 2, 4, P], F32R)
    assert top_of[0] <= nc.sbuf_usable_end
    gt = sb("gt", [P, 2, NTB, AG, TB], at=pick_at)
    top_of[0] = pick_at + 2 * 4 * NTB * AG * TB
    hin = sb("hin", [P, 4, S])
    wgt = sb("wgt", [P, 2, S])
    wgthl = sb("wgthl", [P, 2, 2, S], F32R)
    assert top_of[0] <= nc.sbuf_usable_end
    pos_i = sb("pos_i", [P, TT], I32, at=free)
    pos_f = sb("pos_f", [P, TT], at=free + 32)
    frq = sb("frq", [P, HALF], at=free + 64)
    ang = sb("ang", [P, TT, HALF], at=free + 256)
    turns = sb("turns", [P, TT, HALF], at=free + 512)
    over = sb("over", [P, TT, HALF], at=free + 768)
    c_sig = sb("c_sig", [P, D], at=free + 2048)
    mod0 = sb("mod0", [P, 4, D], at=free + 4 * D + 2048)
    assert free + 4 * D + 2048 + 16 * D <= lat_at
    modv = sb("modv", [P, D], at=free)

    ps = nc.alloc_psum_tensor("ps", [P, 8, S], F32)
    sem = nc.alloc_semaphore

    raw_in = [sem(f"raw_in{i}") for i in range(RAW)]
    hi_done, lo_done, gemm_done = sem("hi_done"), sem("lo_done"), sem("gemm_done")
    mod_done, mod0_done, modv_done, modv_in = sem("mod_done"), sem("mod0_done"), sem("modv_done"), sem("modv_in")
    mod0_in = [sem(f"mod0_in{i}") for i in range(4)]
    bank_free = [sem("bank0_free"), sem("bank1_free")]
    start_in, consts_made, rope_made = sem("start_in"), sem("consts_made"), sem("rope_made")
    c_ready = sem("c_ready")
    params_in, mid_in, keys_in = sem("params_in"), sem("mid_in"), sem("keys_in")
    ws_masked = sem("ws_masked")
    sq_ready, sq_used, ssq_done = sem("sq_ready"), sem("sq_used"), sem("ssq_done")
    root_ready, rstd_ready = sem("root_ready"), sem("rstd_ready")
    t_ready, t_hi, mov_ready = sem("t_ready"), sem("t_hi"), sem("mov_ready")
    lat_norm = sem("lat_norm")
    ln_var, ln_root, ln_ready = sem("ln_var"), sem("ln_root"), sem("ln_ready")
    proj_ready, tok_act, tok_dve = sem("proj_ready"), sem("tok_act"), sem("tok_dve")
    turn_ready, turn_act, turn_dve = sem("turn_ready"), sem("turn_act"), sem("turn_dve")
    side_ready, side_out = sem("side_ready"), sem("side_out")
    qk_ready, max_ready, exp_ready, prob_ready = (
        sem("qk_ready"), sem("max_ready"), sem("exp_ready"), sem("prob_ready"))
    pt_ready, prT_ready, pv_ready, y_ready = sem("pt_ready"), sem("prT_ready"), sem("pv_ready"), sem("y_ready")
    y_hi = sem("y_hi")
    gate_out = [sem(f"gate_out{i}") for i in range(6)]
    gate_in = [sem(f"gate_in{i}") for i in range(6)]
    merged, merged_hi, merged_lo = sem("merged"), sem("merged_hi"), sem("merged_lo")
    score_ready, score_used = sem("score_ready"), sem("score_used")
    h_out = [sem("h_out0"), sem("h_out1")]
    g_sub, g_exp, g_norm = sem("g_sub"), sem("g_exp"), sem("g_norm")
    sel_turned, sel_act, sel_dve = sem("sel_turned"), sem("sel_act"), sem("sel_dve")
    hot_ready, gmm_done, stage_ready = sem("hot_ready"), sem("gmm_done"), sem("stage_ready")
    stage_out = [sem("stage_out0"), sem("stage_out1")]
    gt_in = [sem("gt_in0"), sem("gt_in1")]
    hin_in = [sem(f"hin_in{i}") for i in range(4)]
    w_ready = sem("w_ready")
    v_done, x_added = sem("v_done"), sem("x_added")
    out_ready, out_done = sem("out_ready"), sem("out_done")
    dve_step, setup_step = sem("dve_step"), sem("setup_step")

    def raw_n(m):
        return RAW_OF[("m", m)] if m < M_T else N_HEAD + m - M_T

    def wait_raw(eng, l, m, more=0):
        n = raw_n(m)
        eng.wait_ge(raw_in[n % RAW], l * (16 * RAW_USES) + more * (16 // RAW) + 16 * (n // RAW + 1))

    def split_hi(act, l, m, more=0):
        wait_raw(act, l, m, more)
        act.wait_ge(gemm_done, 1 + l * M_ALL + more + max(m - RING + 1, 0))
        nc.scalar.copy(whl[:, m % RING, 0], raw[:, raw_n(m) % RAW]).then_inc(hi_done, 1)

    def banked(m, l, more_half=0):
        return bank_free[m % 2], 1 + l * N_BANKED + more_half + m // 2 + 1

    def split_lo(dve, l, m, more=0):
        dve.wait_ge(hi_done, l * M_ALL + more + m + 1)
        nc.vector.tensor_tensor(whl[:, m % RING, 1], raw[:, raw_n(m) % RAW],
                                whl[:, m % RING, 0].bitcast(F32), ALU.subtract).then_inc(lo_done, 1)

    def gemm(pe, l, m, src=mov, more=0, more_half=0, rows=None):
        pe.wait_ge(lo_done, 1 + l * M_ALL + more + m + 1)
        pe.wait_ge(bank_free[m % 2], 1 + l * N_BANKED + more_half + m // 2)
        w = whl[:, m % RING]
        for k in range(KC):
            if rows:
                pe.wait_ge(rows[0], rows[1] + k + 1)
            nc.tensor.matmul(ps[:, m % 2], w[:, 0, k], src[:, 0, k], start=(k == 0), stop=False)
            nc.tensor.matmul(ps[:, m % 2], w[:, 0, k], src[:, 1, k], start=False, stop=False)
            mm = nc.tensor.matmul(ps[:, m % 2], w[:, 1, k], src[:, 0, k], start=False, stop=(k == KC - 1))
        mm.then_inc(gemm_done, 1)

    def gemm_tokens(pe, l, m, cols):
        pe.wait_ge(lo_done, 1 + l * M_ALL + m + 1)
        pe.wait_ge(bank_free[m % 2], 1 + l * N_BANKED + m // 2)
        w = whl[:, m % RING]
        for t in range(TT):
            o = ps[:, m % 2, t * P:t * P + cols]
            for k in range(KC):
                hi, lo = mov[:, 0, k, t * P:(t + 1) * P], mov[:, 1, k, t * P:(t + 1) * P]
                nc.tensor.matmul(o, hi, w[:, 0, k, :cols], start=(k == 0), stop=False)
                nc.tensor.matmul(o, hi, w[:, 1, k, :cols], start=False, stop=False)
                mm = nc.tensor.matmul(o, lo, w[:, 0, k, :cols], start=False, stop=(k == KC - 1))
        mm.then_inc(gemm_done, 1)

    def mod_column(column, panel, signal):
        nc.vector.tensor_tensor_reduce(panel, panel, c_act[:], 1.0, 0.0, ALU.mult, ALU.add, column
                                       ).then_inc(signal, 1)

    SQ_H1, SQ_LAT, SQ_H2, SQ_ALL = 0, KC, KC + 5, 2 * KC + 5

    def square(act, l, q, src):
        act.wait_ge(sq_used, 1 + l * SQ_ALL + max(q - 1, 0))
        nc.scalar.activation(sq[:, q % 2], src, ACT.Square).then_inc(sq_ready, 1)

    def sum_squares(pe, l, q, bank, first, last):
        pe.wait_ge(sq_ready, l * SQ_ALL + q + 1)
        mm = nc.tensor.matmul(ps[:, bank], ones[:], sq[:, q % 2], start=first, stop=last)
        mm.then_inc(sq_used, 1)
        return mm

    def rstd(dve, l, k):
        dve.wait_ge(root_ready, l * 4 + k + 1)
        nc.vector.reciprocal(root[:], root[:]).then_inc(rstd_ready, 1)

    SSQ_BANK = (2, 2, 3, 2)

    def take_root(act, l, k, width):
        act.wait_ge(sq_used, 1 + l * SQ_ALL + (SQ_H1 + KC, SQ_LAT + 3, SQ_LAT + 5, SQ_ALL)[k])
        if k == 2:
            act.wait_ge(lat_norm, l * 5 + 3)
        elif k:
            act.wait_ge(mov_ready, l * (3 * KC) + (KC, None, 2 * KC)[k - 1])
        nc.scalar.activation(root[:], ps[:, SSQ_BANK[k]], ACT.Sqrt, bias=eps[:], scale=1.0 / width
                             ).then_inc(root_ready, 1)

    def settle(eng):
        eng.nop(nofuse=True)

    block = nc.Block()
    block.__enter__()

    primed = [gemm_done, lo_done, *bank_free, sq_used, tok_act, tok_dve, turn_act, turn_dve, side_out,
              exp_ready, prT_ready, y_ready, pt_ready, score_ready, score_used, stage_ready, gmm_done]

    N_START, N_PARAMS, N_MID = 5, 6, 3

    @block.sync
    def _(sp):
        for signal in primed:
            sp.sem_inc(signal, 1)
        sp.wait_ge(start_in, 16 * N_START)
        sp.sem_inc(x_added, KC)
        def load(l, n, src, freed=None):
            slot = n % RAW
            if freed is None:
                if n < RAW:
                    sp.wait_ge(lo_done, 1 + l * M_ALL)
                else:
                    kind, i = ORDER[n - RAW]
                    if kind == "mod":
                        sp.wait_ge(mod_done, l * N_MODX + i - MOD_FIRST + 1)
                    else:
                        sp.wait_ge(lo_done, 1 + l * M_ALL + i + 1)
            sp.dma_start(raw[:, slot], src).then_inc(raw_in[slot], 16)

        def panel(table, at):
            return table[ds(at, 1)].rearrange("o p (k c) -> p (o k) c", k=KC)

        for i in range(MOD_FIRST):
            if i >= 4:
                sp.wait_ge(mod0_done, i - 3)
            sp.dma_start(mod0[:, i % 4], w_mod[i]).then_inc(mod0_in[i % 4], 16)
        with sp.Fori(0, DEPTH) as l:
            for n, (kind, i) in enumerate(ORDER):
                if kind == "mod":
                    src = w_mod[ds(l * N_MOD + i, 1)].rearrange("o p (k c) -> p (o k) c", k=KC)
                elif i < M_ABC:
                    src = panel(w_in, l * N_IN + i)
                elif i < M_WO:
                    src = panel(w_abc, l * KC + (i - M_ABC))
                else:
                    src = panel(w_o, l * KC + (i - M_WO))
                load(l, n, src)
            settle(sp)
            with sp.Fori(0, PH) as h:
                for j in range(2 + T_U):
                    src = panel(w_pq, l * 2 * PH + h * 2 + j) if j < 2 else \
                        panel(uT_tab, l * P + h * T_U + (j - 2))
                    sp.wait_ge(lo_done, 1 + l * M_ALL + h * (2 + T_U) + (M_T + j - RAW + 1))
                    load(l, N_HEAD + j, src, freed=True)

            def run(first_m, first_a, times, table):
                settle(sp)
                with sp.Fori(0, times) as i:
                    for j in range(4):
                        sp.wait_ge(lo_done, 1 + l * M_ALL + i * 4 + (first_m + j - RAW + 1))
                        load(l, raw_n(first_m + j), panel(table, l * P + i * 4 + (first_a + j)), freed=True)

            run(M_R1, A_R1, (M_V - M_R1) // 4, uT_tab)
            run(M_V, 0, P // 4, v_tab)

    @block.gpsimd
    def _(pool):
        pool.dma_start(c_act[:], c.to_broadcast([P, D])).then_inc(start_in, 16)
        pool.dma_start(x_sb[:], xT).then_inc(start_in, 16)
        pool.dma_start(pos_i[:], pos).then_inc(start_in, 16)
        pool.dma_start(frq[:], freq).then_inc(start_in, 16)
        pool.dma_start(fin[:], fin_gain).then_inc(start_in, 16)
        nc.gpsimd.memset(ones[:], 1.0)
        nc.gpsimd.memset(eps[:], EPS)
        nc.gpsimd.memset(zeros[:].bitcast(F32), 0.0)
        nc.gpsimd.memset(causal[:], 0.0)
        nc.gpsimd.memset(ident[:], 0.0).then_inc(consts_made, 1)
        pool.wait_ge(consts_made, 1)
        nc.gpsimd.affine_select(out=ident[:], in_=ident[:], compare_op=ALU.not_equal, fill=1.0, base=0,
                                pattern=[[1, P]], channel_multiplier=-1)
        nc.gpsimd.affine_select(out=causal[:], in_=causal[:], compare_op=ALU.is_ge, fill=-1.0e30, base=0,
                                pattern=[[-1, P]], channel_multiplier=1)
        nc.gpsimd.iota(iota[:], [[1, P]], base=0, channel_multiplier=0,
                       allow_small_or_imprecise_dtypes=True).then_inc(consts_made, 1)
        pool.wait_ge(consts_made, 2)
        for half in range(2):
            pool.dma_start(h_d[half, 0:1, :16], ones[0:1, :16]).then_inc(h_out[half], 16)
            pool.dma_start(g_d[half, 0:1, 0, :16], ones[0:1, :16]).then_inc(stage_out[half], 16)
        with pool.Fori(0, DEPTH) as l:
            pool.wait_ge(rope_made, 1)
            one = lambda t: t[ds(l, 1)].rearrange("o p n -> p (o n)")
            pool.dma_start(bmod[:], one(b_mod)).then_inc(params_in, 16)
            pool.dma_start(gain[:], one(qkv_gain)).then_inc(params_in, 16)
            pool.dma_start(uq[:].rearrange("p a b -> p (a b)"), one(w_uq)).then_inc(params_in, 16)
            pool.dma_start(pscale[:], one(pool_scale)).then_inc(params_in, 16)
            pool.dma_start(wpl[:].rearrange("p a b -> p (a b)"), one(w_pool)).then_inc(params_in, 16)
            pool.wait_ge(x_added, l * KC + KC)
            settle(pool)
            pool.dma_start(ukv[:].rearrange("p a b -> p (a b)"), one(w_ukv)).then_inc(params_in, 16)
            for j in range(3 * KC):
                if j == 0:
                    pool.wait_ge(proj_ready, l * 2 * TT + 2 * TT)
                    settle(pool)
                    pool.dma_start(wsT[:].rearrange("p a b -> p (a b)"), one(w_sT)).then_inc(mid_in, 16)
                    pool.dma_start(bsb[:].rearrange("p a b -> p (a b)"),
                                   b_s[ds(l, 1)].to_broadcast([P, 4 * P])).then_inc(mid_in, 16)
                    pool.dma_start(band[:], bands).then_inc(mid_in, 16)
                    pool.wait_ge(mid_in, l * (16 * N_MID) + 16 * N_MID)
                    settle(pool)
                    nc.gpsimd.affine_select(out=wsT[:], in_=wsT[:], compare_op=ALU.is_ge, fill=0.0, base=0,
                                            pattern=[[0, 4], [1, P]], channel_multiplier=-1
                                            ).then_inc(ws_masked, 1)
                pool.wait_ge(*banked(P_GATE + j, l))
                settle(pool)
                pool.dma_start(gate_d[j], gst[:, j % 6]).then_inc(gate_out[j % 6], 16)
            for j in range(3 * KC):
                if j < 6:
                    pool.wait_ge(gate_out[j], l * 64 + 64)
                else:
                    pool.wait_ge(merged, l * KC + j // 3 - 1)
                settle(pool)
                pool.dma_start(gst[:, j % 6], gate_d[j]).then_inc(gate_in[j % 6], 16)
            pool.wait_ge(merged, l * KC + KC)
            pool.wait_ge(gemm_done, 1 + l * M_ALL + M_T)
            settle(pool)
            pool.dma_start(keys[:].rearrange("p a b -> p (a b)"), one(keysT)).then_inc(keys_in, 16)

            def store_h(a, more, slot, m, more_m):
                pool.wait_ge(*banked(m, l, more_m))
                settle(pool)
                pool.dma_start(h_d[ds(more + a, 1)].rearrange("o p t -> p (o t)"), hst[:, slot]
                               ).then_inc(h_out[slot], 16)

            settle(pool)
            with pool.Fori(0, PH) as h:
                for j in range(T_U):
                    store_h(j, h * T_U, j % 2, M_T + 2 + j, h * ((2 + T_U) // 2))
            settle(pool)
            with pool.Fori(0, REST // 4) as i:
                for j in range(4):
                    store_h(A_R1 + j, i * 4, j % 2, M_R1 + j, i * 2)
            settle(pool)
            with pool.Fori(0, NTB // 2) as b:
                for half in range(2):
                    for j in range(BLK_U):
                        store_h(A_G + half * BLK_U + j, b * (2 * BLK_U), j % 2,
                                M_G + half * BLK_U + j, b * BLK_U)
                    pool.wait_ge(stage_ready, 1 + l * (8 * NTB) + b * 16 + half * 8 + 8)
                    settle(pool)
                    pool.dma_start(
                        g_d[:, :, ds(b * 2 + half, 1)].rearrange("a p o x -> p a (o x)"),
                        stage[:, half].rearrange("p (g a) t -> p g (a t)", a=AG)).then_inc(stage_out[half], 16)
            settle(pool)
            with pool.Fori(0, REST // 4) as i:
                for j in range(4):
                    store_h(A_R2 + j, i * 4, j % 2, M_R2 + j, i * 2)
            for half in range(2):
                pool.wait_ge(stage_out[half], 16 + l * (8 * NTB) + 8 * NTB)
                pool.wait_ge(h_out[half], 16 + l * (8 * P) + 8 * P)
            def load_g(half, block_at):
                settle(pool)
                pool.dma_start(gt[:, half].rearrange("p b a t -> p (b a t)"),
                               g_d[ds(block_at, 1)].rearrange("o p b x -> p (o b x)")).then_inc(gt_in[half], 16)

            def load_h(slot, a):
                settle(pool)
                pool.dma_start(hin[:, slot], h_d[ds(a, 1)].rearrange("o p t -> p (o t)")).then_inc(hin_in[slot], 16)

            def load_mod(i):
                settle(pool)
                pool.dma_start(modv[:], w_mod[ds((l + 1) * N_MOD + i, 1)].rearrange("o p k -> p (o k)")
                               ).then_inc(modv_in, 16)

            for half in range(2):
                load_g(half, half)
            for j in range(4):
                load_h(j, j)
            load_mod(0)
            settle(pool)
            with pool.Fori(0, P // 8 - 1) as i:
                for half in range(2):
                    for j in range(4):
                        pool.wait_ge(w_ready, l * P + i * 8 + (half * 4 + j + 1))
                        load_h(j, i * 8 + (half * 4 + j + 4))
                    load_g(half, i * 2 + (half + 2))
                pool.wait_ge(modv_done, l * MOD_FIRST + i + 1)
                load_mod(i + 1)
            for j in range(4):
                pool.wait_ge(w_ready, l * P + (P - 8 + j + 1))
                load_h(j, P - 4 + j)
        pool.wait_ge(out_ready, KC)
        settle(pool)
        pool.dma_start(out, x_sb[:]).then_inc(out_done, 16)
        pool.wait_ge(out_done, 16)

    @block.tensor
    def _(pe):
        pe.wait_ge(consts_made, 2)
        with pe.Fori(0, DEPTH) as l:
            for q in range(KC):
                if q == 0:
                    pe.wait_ge(x_added, l * KC + 3)
                sum_squares(pe, l, SQ_H1 + q, 2, q == 0, q == KC - 1)
            pe.wait_ge(x_added, l * KC + KC)
            for kind, i in STEPS:
                if kind == "panel":
                    if i == P_KR or P_ZV <= i < P_ZU or P_ZP <= i < P_GATE:
                        gemm_tokens(pe, l, i, ROPE if i == P_KR else P)
                    else:
                        gemm(pe, l, i, rows=(mov_ready, l * 3 * KC) if i == 0 else None)
                elif kind == "ssq":
                    if i == 0:
                        pe.wait_ge(root_ready, l * 4 + 1)
                    sum_squares(pe, l, SQ_LAT + i, 2 if i < 3 else 3, i in (0, 3), i in (2, 4))
                elif kind == "proj":
                    t = i % TT
                    if i == 0:
                        pe.wait_ge(params_in, l * (16 * N_PARAMS) + 16 * N_PARAMS)
                    pe.wait_ge(lat_norm, l * 5 + (3 if i < TT else 5))
                    pe.wait_ge(tok_act, 1 + l * 2 * TT + i)
                    pe.wait_ge(tok_dve, 1 + l * 2 * TT + i)
                    flat = ps[:, 4:6].rearrange("p b n -> p (b n)")
                    w, ks, first, width = (uq, 3, 0, HEADS * QK) if i < TT else (ukv, 2, 3, HEADS * (NOPE + VD))
                    for c0 in range(0, width, S):
                        c1 = min(c0 + S, width)
                        for k in range(ks):
                            mm = nc.tensor.matmul(flat[:, c0:c1], lat[:, first + k, t * P:(t + 1) * P],
                                                  w[:, k, c0:c1], start=(k == 0), stop=(k == ks - 1))
                    mm.then_inc(proj_ready, 1)
                elif kind == "turn":
                    if i == 0:
                        pe.wait_ge(root_ready, l * 4 + 3)
                    pe.wait_ge(tok_act, 1 + l * 2 * TT + i + 1)
                    pe.wait_ge(tok_dve, 1 + l * 2 * TT + i + 1)
                    pe.wait_ge(turn_act, 1 + l * 2 * TT + i)
                    pe.wait_ge(turn_dve, 1 + l * 2 * TT + i)
                    for h in range(HEADS):
                        mm = nc.tensor.transpose(ps[:QK, 2 + h // 4, (h % 4) * P:(h % 4 + 1) * P],
                                                 tok[:, i % 2, h, :], ident[:])
                    mm.then_inc(turn_ready, 1)
                elif kind == "ya":
                    if i == 0:
                        pe.wait_ge(ws_masked, l + 1)
                        pe.wait_ge(ln_ready, l + 1)
                        pe.wait_ge(tok_act, 1 + l * 2 * TT + 2 * TT)
                        pe.wait_ge(tok_dve, 1 + l * 2 * TT + 2 * TT)
                    pe.wait_ge(side_out, 1 + l * 12 + max(i - 1, 0))
                    for n in range(TT):
                        mm = nc.tensor.matmul(ps[:, 4 + i % 2, n * P:(n + 1) * P],
                                              vg[:, n, (i // 2) * P:(i // 2 + 1) * P], wsT[:, i],
                                              start=True, stop=True)
                    mm.then_inc(side_ready, 1)
                elif kind == "win":
                    if i == 0:
                        pe.wait_ge(*banked(P_ZP, l))
                        pe.wait_ge(*banked(P_ZP + 1, l))
                    e = 4 + (i if i < 2 else i + 2)
                    pe.wait_ge(side_out, 1 + l * 12 + e - 1)
                    r0 = 64 * (i % 2)
                    for n in range(TT):
                        o = ps[r0:r0 + 64, 4 + i % 2, n * P:(n + 1) * P]
                        mm = nc.tensor.matmul(o, zp[:, n, i * 64:(i + 1) * 64], band[:, i if n else 8 + i],
                                              start=True, stop=(n == 0))
                        if n:
                            mm = nc.tensor.matmul(o, zp[:, n - 1, i * 64:(i + 1) * 64], band[:, 4 + i],
                                                  start=False, stop=True)
                    mm.then_inc(side_ready, 1)
                elif kind == "pool":
                    e = 6 + (i if i < 2 else i + 2)
                    pe.wait_ge(side_out, 1 + l * 12 + e - 1)
                    r0 = 64 * (i % 2)
                    settle(pe)
                    mm = nc.tensor.matmul(ps[r0:r0 + 64, 4 + i % 2], wpl[r0:r0 + 64, i // 2],
                                          ytmp[r0:r0 + 64, i % 2], start=True, stop=True)
                    mm.then_inc(side_ready, 1)
                elif kind == "qk":
                    h, t = divmod(i, TT)
                    if i == 0:
                        pe.wait_ge(turn_act, 1 + l * 2 * TT + 2 * TT)
                        pe.wait_ge(turn_dve, 1 + l * 2 * TT + 2 * TT)
                    pe.wait_ge(exp_ready, 1 + l * 32 + max(i - 1, 0))
                    n = (t + 1) * P
                    nc.tensor.matmul(ps[:, 2 + i % 2, :n], qT[:QK, h, t * P:n], kT[:QK, h, :n],
                                     start=True, stop=False)
                    nc.tensor.matmul(ps[:, 2 + i % 2, t * P:n], ident[:], causal[:],
                                     start=False, stop=True).then_inc(qk_ready, 1)
                elif kind == "pt":
                    t = i % TT
                    pe.wait_ge(prob_ready, l * 32 + i + 1)
                    pe.wait_ge(side_out, 1 + l * 12 + 12)
                    pe.wait_ge(prT_ready, 1 + l * 32 + max(i - 1, 0))
                    for j in range(t + 1):
                        mm = nc.tensor.transpose(ps[:, 4 + i % 2, j * P:(j + 1) * P],
                                                 pr[:, i % 2, j * P:(j + 1) * P], ident[:])
                    mm.then_inc(pt_ready, 1)
                elif kind == "pv":
                    h, t = divmod(i, TT)
                    r0 = 64 * (h % 2)
                    pe.wait_ge(prT_ready, 1 + l * 32 + i + 1)
                    if t == 0:
                        pe.wait_ge(y_ready, 1 + l * HEADS + max(h - 1, 0))
                    for j in range(t + 1):
                        mm = nc.tensor.matmul(ps[r0:r0 + 64, 6, t * P:(t + 1) * P],
                                              vh[:, j, h * VD:(h + 1) * VD], prT[:, i % 2, j * P:(j + 1) * P],
                                              start=(j == 0), stop=(j == t))
                    mm.then_inc(pv_ready, 1)
            pe.wait_ge(mov_ready, l * 3 * KC + 2 * KC)
            pe.wait_ge(y_ready, 1 + l * HEADS + HEADS)
            pe.wait_ge(prT_ready, 1 + l * 32 + 32)
            pe.wait_ge(exp_ready, 1 + l * 32 + 32)
            for i in range(KC):
                m = M_ABC + i
                pe.wait_ge(lo_done, 1 + l * M_ALL + m + 1)
                pe.wait_ge(bank_free[m % 2], 1 + l * N_BANKED + m // 2)
                w = whl[:, m % RING]
                for k in range(KC):
                    b = (0, 0, 1, 1, 1, 1, 2, 2)[k]
                    first, last = k in (0, 2, 6), k in (1, 5, 7)
                    o = ps[:, (m % 2, 2 + m % 2, 4 + m % 2)[b]]
                    nc.tensor.matmul(o, w[:, 0, k], mov[:, 0, k], start=first, stop=False)
                    nc.tensor.matmul(o, w[:, 0, k], mov[:, 1, k], start=False, stop=False)
                    mm = nc.tensor.matmul(o, w[:, 1, k], mov[:, 0, k], start=False, stop=last)
                mm.then_inc(gemm_done, 1)
            for i in range(KC):
                gemm(pe, l, M_WO + i, src=mrg, rows=(merged_lo, l * KC) if i == 0 else None)
                if i == 1:
                    pe.wait_ge(merged, l * KC + KC)
                if i:
                    sum_squares(pe, l, SQ_H2 + i - 1, 2, i == 1, False)
            sum_squares(pe, l, SQ_H2 + KC - 1, 2, False, True)
            settle(pe)
            with pe.Fori(0, PH) as h:
                for j in range(2 + T_U):
                    m = M_T + j
                    gemm(pe, l, m, more=h * (2 + T_U), more_half=h * ((2 + T_U) // 2),
                         rows=None if j else (mov_ready, l * 3 * KC + 2 * KC))
                    if j in (2, 3):
                        side = j - 2
                        if side == 0:
                            pe.wait_ge(keys_in, l * 16 + 16)
                        pe.wait_ge(*banked(M_T + side, l, h * ((2 + T_U) // 2)))
                        pe.wait_ge(score_used, 1 + l * 2 * PH + h * 2 + side)
                        for t in range(TT):
                            mm = nc.tensor.matmul(ps[:, 2 + side, t * P:(t + 1) * P],
                                                  qh[:, side, t * P:(t + 1) * P],
                                                  keys[:, ds(h * 2 + side, 1)].rearrange("p o k -> p (o k)"),
                                                  start=True, stop=True)
                        mm.then_inc(score_ready, 1)

            def experts(first_m, times):
                settle(pe)
                with pe.Fori(0, times) as i:
                    for j in range(4):
                        gemm(pe, l, first_m + j, more=i * 4, more_half=i * 2)

            experts(M_R1, REST // 4)
            pe.wait_ge(score_used, 1 + l * 2 * PH + 2 * PH)
            pe.wait_ge(g_norm, l + 1)
            for b, src in ((2, sel1), (3, sel2), (4, topv)):
                for t in range(TT):
                    mm = nc.tensor.transpose(ps[:, b, t * P:(t + 1) * P],
                                             src[:, t].rearrange("p h k -> p (h k)"), ident[:])
            mm.then_inc(sel_turned, 1)
            pe.wait_ge(sel_dve, l + 1)
            settle(pe)
            with pe.Fori(0, NTB // 2) as b:
                for half in range(2):
                    for j in range(BLK_U):
                        jj = half * BLK_U + j
                        gemm(pe, l, M_G + jj, more=b * (2 * BLK_U), more_half=b * BLK_U)
                        for s in range(2 * j, 2 * j + 2):
                            e = half * 8 + s
                            pe.wait_ge(hot_ready, l * (8 * NTB) + b * 16 + e + 1)
                            if e < 4:
                                pe.wait_ge(stage_ready, 1 + l * (8 * NTB) + b * 16)
                            else:
                                pe.wait_ge(stage_ready, 1 + l * (8 * NTB) + b * 16 + (e - 3))
                            for t in range(4):
                                o = ps[:, 4 + e % 4, t * P:(t + 1) * P]
                                nc.tensor.matmul(o, hot2[:, e % 2, t], hotg[:, e % 2, 0, t], start=True, stop=False)
                                mm = nc.tensor.matmul(o, hot2[:, e % 2, t], hotg[:, e % 2, 1, t],
                                                      start=False, stop=True)
                            mm.then_inc(gmm_done, 1)
            experts(M_R2, REST // 4)
            pe.wait_ge(bank_free[0], 1 + l * N_BANKED + N_BANKED)
            pe.wait_ge(bank_free[1], 1 + l * N_BANKED + N_BANKED)
            pe.wait_ge(sel_act, l + 1)
            pe.wait_ge(stage_ready, 1 + l * (8 * NTB) + 8 * NTB)
            for c in range(KC):
                nc.tensor.matmul(ps[:, c], zeros[:], mov[:, 0, 0], start=True, stop=False)
            settle(pe)
            with pe.Fori(0, P // 4) as i:
                for j in range(4):
                    pe.wait_ge(lo_done, 1 + l * M_ALL + i * 4 + (M_V + j + 1))
                    pe.wait_ge(w_ready, l * P + i * 4 + (j + 1))
                    w = whl[:, (M_V + j) % RING]
                    for c in range(KC):
                        nc.tensor.matmul(ps[:, c], w[:, 0, c], wgthl[:, j % 2, 0], start=False, stop=False)
                        nc.tensor.matmul(ps[:, c], w[:, 0, c], wgthl[:, j % 2, 1], start=False, stop=False)
                        mm = nc.tensor.matmul(ps[:, c], w[:, 1, c], wgthl[:, j % 2, 0], start=False, stop=False)
                    mm.then_inc(gemm_done, 1)
            for c in range(KC):
                nc.tensor.matmul(ps[:, c], zeros[:], mov[:, 0, 0], start=False, stop=True).then_inc(v_done, 1)
        pe.wait_ge(x_added, DEPTH * KC + 3)
        for q in range(KC):
            sum_squares(pe, DEPTH, q, 2, q == 0, q == KC - 1)

    @block.scalar
    def _(act):
        act.wait_ge(start_in, 16 * N_START)
        nc.scalar.activation(c_sig[:], c_act[:], ACT.Sigmoid).then_inc(c_ready, 1)
        act.wait_ge(rope_made, 1)
        nc.scalar.activation(sin[:], ang[:], ACT.Sin)
        nc.scalar.activation(cos[:], over[:], ACT.Sin).then_inc(rope_made, 1)

        def norm_h(l, which):
            for q in range(KC if which == 0 else 0):
                act.wait_ge(x_added, l * KC + q + 1)
                square(act, l, SQ_H1 + q, x_sb[:, q])
            take_root(act, l, 3 * which, D)
            if not which:
                for m in range(LEAD):
                    split_hi(act, l, m)
            sh = (0, 3 * KC)[which]
            for c in range(KC):
                act.wait_ge(t_ready, l * 2 * KC + which * KC + c + 1)
                nc.scalar.activation(mov[:, 0, c], ht[:, c % 2], ACT.Identity, bias=mod[:, sh + c:sh + c + 1]
                                     ).then_inc(t_hi, 1)

        with act.Fori(0, DEPTH) as l:
            act.wait_ge(consts_made, 2)
            norm_h(l, 0)
            for kind, i in STEPS:
                if kind == "panel":
                    split_hi(act, l, i + LEAD)
                    bank = ps[:, i % 2]
                    tiles = bank.rearrange("p (t c) -> p t c", t=TT)
                    if i == P_KR:
                        continue
                    act.wait_ge(gemm_done, 1 + l * M_ALL + i + 1)
                    if i < P_KR:
                        square(act, l, SQ_LAT + i, bank)
                        nc.scalar.copy(lat[:, i], bank).then_inc(bank_free[i % 2], 1)
                    elif i < P_ZU:
                        j = i - P_ZV
                        nc.scalar.activation(vg[:, :, j * P:(j + 1) * P], tiles, ACT.Gelu_apprx_tanh
                                             ).then_inc(bank_free[i % 2], 1)
                    elif i < P_ZP:
                        nc.scalar.activation(ug[:, i - P_ZU], bank, ACT.Gelu_apprx_tanh
                                             ).then_inc(bank_free[i % 2], 1)
                    elif i < P_GATE:
                        j = i - P_ZP
                        nc.scalar.copy(zp[:, :, j * P:(j + 1) * P], tiles).then_inc(bank_free[i % 2], 1)
                    else:
                        j = i - P_GATE
                        if j == 0:
                            act.wait_ge(proj_ready, l * 2 * TT + TT)
                        if j >= 6:
                            act.wait_ge(gate_out[j % 6], l * 64 + 16 * (j // 6))
                        nc.scalar.activation(gst[:, j % 6], bank, ACT.Sigmoid).then_inc(bank_free[i % 2], 1)
                elif kind == "root":
                    take_root(act, l, 1 + i, (Q_LORA, KV_LORA)[i])
                elif kind == "proj":
                    act.wait_ge(proj_ready, l * 2 * TT + i + 1)
                    if i >= 2:
                        act.wait_ge(turn_ready, l * 2 * TT + i - 1)
                    flat = ps[:, 4:6].rearrange("p b n -> p (b n)")
                    if i < TT:
                        nc.scalar.copy(tok[:, i % 2, :, :NOPE],
                                       flat[:, :HEADS * QK].rearrange("p (h c) -> p h c", c=QK)[:, :, :NOPE]
                                       ).then_inc(tok_act, 1)
                    else:
                        kv = flat.rearrange("p (h c) -> p h c", c=NOPE + VD)
                        nc.scalar.copy(tok[:, i % 2, :, :NOPE], kv[:, :, :NOPE])
                        nc.scalar.copy(vh[:, i - TT].rearrange("p (h c) -> p h c", c=VD), kv[:, :, NOPE:]
                                       ).then_inc(tok_act, 1)
                elif kind == "turn":
                    act.wait_ge(turn_ready, l * 2 * TT + i + 1)
                    dst, t = (qT if i < TT else kT), i % TT
                    nc.scalar.copy(dst[:QK, 0:4, t * P:(t + 1) * P],
                                   ps[:QK, 2].rearrange("p (h t) -> p h t", h=4)).then_inc(turn_act, 1)
                elif kind == "ya" and i == 0:
                    act.wait_ge(ln_var, l + 1)
                    nc.scalar.activation(lnr[:], bn2[:, :, 1], ACT.Sqrt, bias=eps[:]).then_inc(ln_root, 1)
                elif kind == "qk":
                    n = (i % TT + 1) * P
                    act.wait_ge(max_ready, l * 32 + i + 1)
                    act.wait_ge(pt_ready, 1 + l * 32 + max(i - 1, 0))
                    act.wait_ge(side_ready, l * 12 + 12)
                    nc.scalar.activation(pr[:, i % 2, :n], ps[:, 2 + i % 2, :n], ACT.Exp,
                                         bias=nmx[:, i % 2:i % 2 + 1], scale=SCALE,
                                         accum_out=rsum[:, i % 2:i % 2 + 1]).then_inc(exp_ready, 1)
            for k in range(KC):
                if k == 0:
                    act.wait_ge(gemm_done, 1 + l * M_ALL + N_IN)
                    act.wait_ge(y_ready, 1 + l * HEADS + HEADS)
                    act.wait_ge(side_out, 1 + l * 12 + 12)
                nc.scalar.copy(mov[:, 0, k], y[:, k]).then_inc(y_hi, 1)
            for i in range(KC):
                split_hi(act, l, M_ABC + i + LEAD)
                act.wait_ge(merged, l * KC + i + 1)
                if i == 0:
                    act.wait_ge(pv_ready, l * 32 + 32)
                nc.scalar.copy(mrg[:, 0, i], ytmp[:, i % 2]).then_inc(merged_hi, 1)
            for i in range(KC):
                split_hi(act, l, M_WO + i + LEAD)
                act.wait_ge(*banked(M_WO + i, l))
                square(act, l, SQ_H2 + i, x_sb[:, i])
            norm_h(l, 1)

            def post_u(a, more, m, more_m):
                act.wait_ge(gemm_done, 1 + l * M_ALL + more_m + m + 1)
                act.wait_ge(h_out[a % 2], 16 + l * (8 * P) + more * 8 + 16 * (a // 2))
                nc.scalar.activation(hst[:, a % 2], ps[:, m % 2], ACT.Gelu_apprx_tanh
                                     ).then_inc(bank_free[m % 2], 1)

            settle(act)
            with act.Fori(0, PH) as h:
                for j in range(2 + T_U):
                    m, more = M_T + j, h * (2 + T_U)
                    split_hi(act, l, m + LEAD, more)
                    if j < 2:
                        act.wait_ge(gemm_done, 1 + l * M_ALL + more + m + 1)
                        act.wait_ge(score_ready, 1 + l * 2 * PH + h * 2)
                        nc.scalar.copy(qh[:, j], ps[:, m % 2]).then_inc(bank_free[m % 2], 1)
                    else:
                        post_u(j - 2, h * T_U, m, more)

            def experts(first_m, first_a, times):
                settle(act)
                with act.Fori(0, times) as i:
                    for j in range(4):
                        split_hi(act, l, first_m + j + LEAD, i * 4)
                        post_u(first_a + j, i * 4, first_m + j, i * 4)

            act.wait_ge(g_sub, l + 1)
            nc.scalar.activation(topv[:], topv[:], ACT.Exp).then_inc(g_exp, 1)
            experts(M_R1, A_R1, REST // 4)
            act.wait_ge(sel_turned, l + 1)
            nc.scalar.copy(sel1T[:], ps[:, 2])
            nc.scalar.copy(sel2T[:], ps[:, 3]).then_inc(sel_act, 1)
            settle(act)
            with act.Fori(0, NTB // 2) as b:
                for half in range(2):
                    for j in range(BLK_U):
                        jj = half * BLK_U + j
                        split_hi(act, l, M_G + jj + LEAD, b * (2 * BLK_U))
                        post_u(A_G + jj, b * (2 * BLK_U), M_G + jj, b * (2 * BLK_U))
                        for s in range(2 * j, 2 * j + 2):
                            e = half * 8 + s
                            act.wait_ge(gmm_done, 1 + l * (8 * NTB) + b * 16 + e + 1)
                            if s == 0:
                                act.wait_ge(stage_out[half], 16 + l * (8 * NTB) + b * 16)
                            nc.scalar.copy(stage[:, half, :, 4 * s:4 * s + 4].rearrange("p a t -> p t a"),
                                           ps[:, 4 + e % 4].rearrange("p (t a) -> p t a", t=4)
                                           ).then_inc(stage_ready, 1)
            experts(M_R2, A_R2, REST // 4)
            settle(act)
            with act.Fori(0, P // 4 - 1) as i:
                for j in range(4):
                    split_hi(act, l, M_V + j + LEAD, i * 4)
            for j in range(RING - LEAD):
                split_hi(act, l, M_ALL - (RING - LEAD) + j)
        for q in range(KC):
            act.wait_ge(x_added, DEPTH * KC + q + 1)
            square(act, DEPTH, q, x_sb[:, q])
        take_root(act, DEPTH, 0, D)

    @block.vector
    def _(dve):
        chain = Chain(dve, dve_step, dve_chain)
        dve.wait_ge(start_in, 16 * N_START)
        dve.wait_ge(c_ready, 1)
        nc.vector.tensor_tensor(c_act[:], c_act[:], c_sig[:], ALU.mult).then_inc(c_ready, 1)
        setup = Chain(dve, setup_step, 0)
        setup.link(nc.vector.tensor_copy(pos_f[:], pos_i[:]))
        for t in range(TT):
            last = nc.vector.tensor_scalar(ang[:, t], frq[:], pos_f[:, t:t + 1], None, ALU.mult)
        setup.link(last)
        magic, tau = 12582912.0, 2 * np.pi
        parts = [6.28125, 0.0019340515136718750]
        parts.append(tau - sum(parts))
        setup.link(nc.vector.tensor_scalar(turns[:], ang[:], 1.0 / tau, magic, ALU.mult, ALU.add))
        setup.link(nc.vector.tensor_scalar(turns[:], turns[:], magic, None, ALU.subtract))
        for part in parts:
            setup.link(nc.vector.scalar_tensor_tensor(ang[:], turns[:], -part, ang[:], ALU.mult, ALU.add))
        below = float(np.nextafter(np.float32(np.pi), np.float32(0)))
        setup.link(nc.vector.tensor_scalar(over[:], ang[:], float(np.pi / 2), None, ALU.add))
        setup.link(nc.vector.tensor_scalar(turns[:], over[:], below, -tau, ALU.is_gt, ALU.mult))
        setup.link(nc.vector.tensor_tensor(over[:], over[:], turns[:], ALU.add))
        setup.link(nc.vector.tensor_scalar(over[:], over[:], below, -below, ALU.min, ALU.max))
        nc.vector.tensor_scalar(ang[:], ang[:], below, -below, ALU.min, ALU.max).then_inc(rope_made, 1)

        dve.wait_ge(c_ready, 2)
        for i in range(MOD_FIRST):
            dve.wait_ge(mod0_in[i % 4], 16 * (i // 4 + 1))
            mod_column(mod[:, i:i + 1], mod0[:, i % 4], mod0_done)
        dve.wait_ge(mod0_done, MOD_FIRST)

        def norm_h(l, which):
            rstd(dve, l, 3 * which)
            dve.wait_ge(rstd_ready, l * 4 + 3 * which + 1)
            if not which:
                for m in range(LEAD):
                    split_lo(dve, l, m)
            sh, sc = (0, 3 * KC)[which], (KC, 4 * KC)[which]
            for c in range(KC + 1):
                if c < KC:
                    n = which * KC + c
                    if c >= 2:
                        dve.wait_ge(mov_ready, l * 3 * KC + (0, 2 * KC)[which] + c - 1)
                    nc.vector.scalar_tensor_tensor(ht[:, c % 2], x_sb[:, c], mod[:, sc + c:sc + c + 1], root[:],
                                                   ALU.mult, ALU.mult).then_inc(t_ready, 1)
                if c:
                    n = which * KC + c - 1
                    dve.wait_ge(t_hi, l * 2 * KC + n + 1)
                    nc.vector.scalar_tensor_tensor(mov[:, 1, c - 1], ht[:, (c - 1) % 2],
                                                   mod[:, sh + c - 1:sh + c], mov[:, 0, c - 1].bitcast(F32),
                                                   ALU.add, ALU.subtract).then_inc(mov_ready, 1)

        with dve.Fori(0, DEPTH) as l:
            chain.start(l)
            dve.wait_ge(params_in, l * (16 * N_PARAMS) + 16 * N_PARAMS)
            chain.link(nc.vector.tensor_tensor(mod[:, :MOD_FIRST], mod[:, :MOD_FIRST], bmod[:, :MOD_FIRST], ALU.add))
            chain.link(nc.vector.tensor_scalar(mod[:, KC:2 * KC], mod[:, KC:2 * KC], 1.0, None, ALU.add))
            norm_h(l, 0)
            for kind, i in STEPS:
                if kind == "panel":
                    split_lo(dve, l, i + LEAD)
                    if i == P_KR:
                        dve.wait_ge(gemm_done, 1 + l * M_ALL + i + 1)
                        nc.vector.tensor_copy(kr[:], ps[:, i % 2].rearrange("p (t c) -> p t c", t=TT)[:, :, :ROPE]
                                              ).then_inc(bank_free[i % 2], 1)
                    if i == P_ZU:
                        dve.wait_ge(bank_free[0], 1 + l * N_BANKED + P_ZV // 2 + 1)
                        dve.wait_ge(bank_free[1], 1 + l * N_BANKED + (P_ZV + 1) // 2 + 1)
                        settle(dve)
                        for t in range(TT):
                            last = nc.vector.bn_stats(bn6[:, t], vg[:, t])
                        chain.link(last)
                        settle(dve)
                        for t in range(TT):
                            last = nc.vector.bn_aggr(bn2[:, t], bn6[:, t])
                        last.then_inc(ln_var, 1)
                    if i < N_MODX:
                        n = RAW_OF[("mod", MOD_FIRST + i)]
                        dve.wait_ge(raw_in[n % RAW], l * (16 * RAW_USES) + 16 * (n // RAW + 1))
                        mod_column(mod[:, MOD_FIRST + i:MOD_FIRST + i + 1],
                                   raw[:, n % RAW].rearrange("p k c -> p (k c)"), mod_done)
                    if i == N_MODX:
                        dve.wait_ge(mod_done, l * N_MODX + N_MODX)
                        chain.link(nc.vector.tensor_tensor(mod[:, MOD_FIRST:], mod[:, MOD_FIRST:],
                                                           bmod[:, MOD_FIRST:], ALU.add))
                        chain.link(nc.vector.tensor_scalar(mod[:, 4 * KC:5 * KC], mod[:, 4 * KC:5 * KC], 1.0, None,
                                                           ALU.add))
                elif kind == "root":
                    rstd(dve, l, 1 + i)
                    dve.wait_ge(rstd_ready, l * 4 + 2 + i)
                    for k in ((0, 1, 2), (3, 4))[i]:
                        dve.wait_ge(*banked(k, l))
                        nc.vector.scalar_tensor_tensor(lat[:, k], lat[:, k], gain[:, k:k + 1], root[:],
                                                       ALU.mult, ALU.mult).then_inc(lat_norm, 1)
                elif kind == "proj":
                    t = i % TT
                    dve.wait_ge(proj_ready, l * 2 * TT + i + 1)
                    if i == 0:
                        dve.wait_ge(rope_made, 2)
                    if i < TT:
                        src = ps[:, 4:6].rearrange("p b n -> p (b n)")[:, :HEADS * QK].rearrange(
                            "p (h c) -> p h c", c=QK)[:, :, NOPE:]
                        n = HEADS
                        dve.wait_ge(tok_act, 1 + l * 2 * TT + i + 1)
                    else:
                        src, n = kr[:, t:t + 1], 1
                        if i == TT:
                            dve.wait_ge(bank_free[P_KR % 2], 1 + l * N_BANKED + P_KR // 2 + 1)
                    x1, x2 = src[:, :, :HALF], src[:, :, HALF:]
                    cs = cos[:, t:t + 1].to_broadcast([P, n, HALF])
                    sn = sin[:, t:t + 1].to_broadcast([P, n, HALF])
                    nc.vector.tensor_tensor(rt[:, 0, :n], x1, cs, ALU.mult)
                    nc.vector.tensor_tensor(rt[:, 1, :n], x2, sn, ALU.mult)
                    nc.vector.tensor_tensor(rt[:, 2, :n], x2, cs, ALU.mult)
                    chain.link(nc.vector.tensor_tensor(rt[:, 3, :n], x1, sn, ALU.mult))
                    if i >= 2:
                        dve.wait_ge(turn_ready, l * 2 * TT + i - 1)
                    dst = tok[:, i % 2, :, NOPE:]
                    if i < TT:
                        nc.vector.tensor_tensor(dst[:, :, :HALF], rt[:, 0], rt[:, 1], ALU.subtract)
                        nc.vector.tensor_tensor(dst[:, :, HALF:], rt[:, 2], rt[:, 3], ALU.add).then_inc(tok_dve, 1)
                        dve.wait_ge(tok_dve, 1 + l * 2 * TT + i + 1)
                    else:
                        a, b, c, d = (rt[:, j, :1].to_broadcast([P, HEADS, HALF]) for j in range(4))
                        nc.vector.tensor_tensor(dst[:, :, :HALF], a, b, ALU.subtract)
                        nc.vector.tensor_tensor(dst[:, :, HALF:], c, d, ALU.add).then_inc(tok_dve, 1)
                        dve.wait_ge(tok_dve, 1 + l * 2 * TT + i + 1)
                elif kind == "turn":
                    dve.wait_ge(turn_ready, l * 2 * TT + i + 1)
                    dst, t = (qT if i < TT else kT), i % TT
                    nc.vector.tensor_copy(dst[:QK, 4:8, t * P:(t + 1) * P],
                                          ps[:QK, 3].rearrange("p (h t) -> p h t", h=4)).then_inc(turn_dve, 1)
                    if i == 2 * TT - 1:
                        dve.wait_ge(ln_root, l + 1)
                        chain.link(nc.vector.reciprocal(lnr[:], lnr[:]))
                        for t in range(TT):
                            last = nc.vector.tensor_scalar(vg[:, t], vg[:, t], bn2[:, t, 0:1], lnr[:, t:t + 1],
                                                           ALU.subtract, ALU.mult)
                        last.then_inc(ln_ready, 1)
                elif kind == "ya":
                    dve.wait_ge(side_ready, l * 12 + i + 1)
                    if i == 0:
                        dve.wait_ge(mid_in, l * (16 * N_MID) + 16 * N_MID)
                        dve.wait_ge(bank_free[1], 1 + l * N_BANKED + (P_ZU + 1) // 2 + 1)
                        dve.wait_ge(bank_free[0], 1 + l * N_BANKED + P_ZU // 2 + 1)
                    r0 = 64 * (i % 2)
                    chain.link(nc.vector.tensor_tensor(
                        ytmp[r0:r0 + 64, i % 2].rearrange("p (n t) -> p n t", n=TT),
                        ps[r0:r0 + 64, 4 + i % 2].rearrange("p (n t) -> p n t", n=TT),
                        bsb[r0:r0 + 64, i:i + 1].to_broadcast([64, TT, P]), ALU.add))
                    nc.vector.tensor_tensor(y[r0:r0 + 64, i // 2], ytmp[r0:r0 + 64, i % 2], ug[r0:r0 + 64, i // 2],
                                            ALU.mult).then_inc(side_out, 1)
                elif kind == "win":
                    e = 4 + (i if i < 2 else i + 2)
                    r0 = 64 * (i % 2)
                    dve.wait_ge(side_ready, l * 12 + e + 1)
                    dve.wait_ge(side_out, 1 + l * 12 + e)
                    nc.vector.tensor_copy(ytmp[r0:r0 + 64, i % 2], ps[r0:r0 + 64, 4 + i % 2]).then_inc(side_out, 1)
                elif kind == "pool":
                    e = 6 + (i if i < 2 else i + 2)
                    r0 = 64 * (i % 2)
                    dve.wait_ge(side_ready, l * 12 + e + 1)
                    nc.vector.tensor_scalar(y[r0:r0 + 64, 6 + i // 2], ps[r0:r0 + 64, 4 + i % 2],
                                            pscale[r0:r0 + 64, i // 2:i // 2 + 1], None, ALU.mult
                                            ).then_inc(side_out, 1)
                if kind == "qk":
                    n, b = (i % TT + 1) * P, i % 2
                    dve.wait_ge(qk_ready, l * 32 + i + 1)
                    chain.link(nc.vector.tensor_reduce(mx[:, b:b + 1], ps[:, 2 + b, :n], AX, ALU.max))
                    nc.vector.tensor_scalar(nmx[:, b:b + 1], mx[:, b:b + 1], -SCALE, None, ALU.mult
                                            ).then_inc(max_ready, 1)
                if kind == "pt":
                    n, b = (i % TT + 1) * P, i % 2
                    dve.wait_ge(exp_ready, 1 + l * 32 + i + 1)
                    chain.link(nc.vector.reciprocal(rinv[:, b:b + 1], rsum[:, b:b + 1]))
                    nc.vector.tensor_scalar(pr[:, b, :n], pr[:, b, :n], rinv[:, b:b + 1], None, ALU.mult
                                            ).then_inc(prob_ready, 1)
                    dve.wait_ge(pt_ready, 1 + l * 32 + i + 1)
                    if i >= 2:
                        dve.wait_ge(pv_ready, l * 32 + i - 1)
                    nc.vector.tensor_copy(prT[:, b, :n], ps[:, 4 + b, :n]).then_inc(prT_ready, 1)
                if kind == "pv" and i % TT == TT - 1:
                    h = i // TT
                    r0 = 64 * (h % 2)
                    dve.wait_ge(pv_ready, l * 32 + i + 1)
                    nc.vector.tensor_copy(y[r0:r0 + 64, 2 + h // 2], ps[r0:r0 + 64, 6]).then_inc(y_ready, 1)
            for k in range(KC):
                dve.wait_ge(y_hi, l * KC + k + 1)
                nc.vector.tensor_tensor(mov[:, 1, k], y[:, k], mov[:, 0, k].bitcast(F32), ALU.subtract
                                        ).then_inc(mov_ready, 1)
            for i in range(KC):
                m = M_ABC + i
                split_lo(dve, l, m + LEAD)
                dve.wait_ge(gemm_done, 1 + l * M_ALL + m + 1)
                for b in range(3):
                    j = 3 * i + b
                    dve.wait_ge(gate_in[j % 6], l * 64 + 16 * (j // 6 + 1))
                if i >= 2:
                    dve.wait_ge(merged_lo, l * KC + i - 1)
                g = [gst[:, (3 * i + b) % 6] for b in range(3)]
                for b in range(3):
                    last = nc.vector.tensor_tensor(g[b], ps[:, (m % 2, 2 + m % 2, 4 + m % 2)[b]], g[b], ALU.mult)
                last.then_inc(bank_free[m % 2], 1)
                dve.wait_ge(bank_free[m % 2], 1 + l * N_BANKED + m // 2 + 1)
                chain.link(nc.vector.tensor_tensor(ytmp[:, i % 2], g[0], g[1], ALU.add))
                nc.vector.tensor_tensor(ytmp[:, i % 2], ytmp[:, i % 2], g[2], ALU.add).then_inc(merged, 1)
                dve.wait_ge(merged_hi, l * KC + i + 1)
                nc.vector.tensor_tensor(mrg[:, 1, i], ytmp[:, i % 2], mrg[:, 0, i].bitcast(F32), ALU.subtract
                                        ).then_inc(merged_lo, 1)
            for i in range(KC):
                m = M_WO + i
                split_lo(dve, l, m + LEAD)
                dve.wait_ge(gemm_done, 1 + l * M_ALL + m + 1)
                nc.vector.scalar_tensor_tensor(x_sb[:, i], ps[:, m % 2], mod[:, 2 * KC + i:2 * KC + i + 1],
                                               x_sb[:, i], ALU.mult, ALU.add).then_inc(bank_free[m % 2], 1)
            norm_h(l, 1)

            settle(dve)
            with dve.Fori(0, PH) as h:
                more = h * (2 + T_U)
                chain.enter(h, 21)

                def best(side):
                    dve.wait_ge(score_ready, 1 + l * 2 * PH + h * 2 + side + 1)
                    sc = ps[:, 2 + side].rearrange("p (t k) -> p t k", t=TT)
                    settle(dve)
                    for t in range(TT):
                        last = nc.vector.max(v12[:, t, side, :8], sc[:, t])
                    chain.link(last)
                    settle(dve)
                    for t in range(TT):
                        nc.vector.max_index(i12u[:, t, side, :8], v12[:, t, side, :8], sc[:, t])
                        last = nc.vector.match_replace(sc2[:, t], v12[:, t, side, :8], sc[:, t], NEG)
                    last.then_inc(score_used, 1)
                    dve.wait_ge(score_used, 1 + l * 2 * PH + h * 2 + side + 1)
                    settle(dve)
                    for t in range(TT):
                        last = nc.vector.max(v12[:, t, side, 8:], sc2[:, t])
                    chain.link(last)
                    settle(dve)
                    for t in range(TT):
                        last = nc.vector.max_index(i12u[:, t, side, 8:], v12[:, t, side, 8:], sc2[:, t])
                    chain.link(last)
                    chain.link(nc.vector.tensor_copy(i12[:, :, side], i12u[:, :, side]))

                def pairs():
                    c4 = cand[:].rearrange("p t (a b) -> p t a b", a=TOPK)
                    chain.link(nc.vector.tensor_tensor(
                        c4, v12[:, :, 0].unsqueeze(3).to_broadcast([P, TT, TOPK, TOPK]),
                        v12[:, :, 1].unsqueeze(2).to_broadcast([P, TT, TOPK, TOPK]), ALU.add))
                    settle(dve)
                    for t in range(TT):
                        last = nc.vector.max(topc[:, t, :8], cand[:, t])
                    chain.link(last)
                    settle(dve)
                    for t in range(TT):
                        nc.vector.max_index(posu[:, t, :8], topc[:, t, :8], cand[:, t])
                        last = nc.vector.match_replace(cand2[:, t], topc[:, t, :8], cand[:, t], NEG)
                    chain.link(last)

                def pairs2():
                    settle(dve)
                    for t in range(TT):
                        last = nc.vector.max(topc[:, t, 8:], cand2[:, t])
                    chain.link(last)
                    settle(dve)
                    for t in range(TT):
                        last = nc.vector.max_index(posu[:, t, 8:], topc[:, t, 8:], cand2[:, t])
                    chain.link(last)
                    nc.vector.tensor_copy(topv[:, :, ds(h, 1)].rearrange("p t o k -> p t (o k)"), topc[:])
                    nc.vector.tensor_single_scalar(abu[:, 0], posu[:], 4, ALU.logical_shift_right)
                    chain.link(nc.vector.tensor_single_scalar(abu[:, 1], posu[:], 15, ALU.bitwise_and))
                    chain.link(nc.vector.tensor_copy(abf[:], abu[:]))

                def key_of(side):
                    e3 = eq[:].rearrange("p t k r -> p (t k) r")
                    chain.link(nc.vector.tensor_tensor(
                        e3, abf[:, side].rearrange("p t k -> p (t k)").unsqueeze(2).to_broadcast([P, TT * TOPK, TOPK]),
                        iota[:, :TOPK].unsqueeze(1).to_broadcast([P, TT * TOPK, TOPK]), ALU.is_equal))
                    chain.link(nc.vector.tensor_tensor(
                        eq[:], eq[:], i12[:, :, side].unsqueeze(2).to_broadcast([P, TT, TOPK, TOPK]), ALU.mult))
                    chain.link(nc.vector.tensor_reduce(
                        (sel1, sel2)[side][:, :, ds(h, 1)].rearrange("p t o k -> p t (o k)"), eq[:], AX, ALU.add))

                work = {2: lambda: best(0), 3: lambda: best(1), 4: pairs, 5: pairs2,
                        6: lambda: key_of(0), 7: lambda: key_of(1)}
                for j in range(2 + T_U):
                    split_lo(dve, l, M_T + j + LEAD, more)
                    if j in work:
                        work[j]()
            chain.leave(PH)

            t3 = topv[:].rearrange("p t h k -> p (t h) k")
            chain.link(nc.vector.tensor_copy(den[:], t3[:, :, 0]))
            nc.vector.tensor_tensor(t3, t3, den[:].unsqueeze(2).to_broadcast([P, TT * PH, TOPK]), ALU.subtract
                                    ).then_inc(g_sub, 1)

            def experts(first_m, times):
                settle(dve)
                with dve.Fori(0, times) as i:
                    for j in range(4):
                        split_lo(dve, l, first_m + j + LEAD, i * 4)

            dve.wait_ge(g_exp, l + 1)
            chain.link(nc.vector.tensor_reduce(den[:], t3, AX, ALU.add))
            chain.link(nc.vector.reciprocal(dinv[:], den[:]))
            nc.vector.tensor_tensor(t3, t3, dinv[:].unsqueeze(2).to_broadcast([P, TT * PH, TOPK]), ALU.mult
                                    ).then_inc(g_norm, 1)
            experts(M_R1, REST // 4)
            dve.wait_ge(sel_turned, l + 1)
            chain.link(nc.vector.tensor_copy(gT[:], ps[:, 4]))
            chain.link(nc.vector.tensor_copy(gThl[:, 0], gT[:]))
            nc.vector.tensor_tensor(gThl[:, 1], gT[:], gThl[:, 0].bitcast(F32), ALU.subtract).then_inc(sel_dve, 1)
            dve.wait_ge(sel_dve, l + 1)
            dve.wait_ge(sel_act, l + 1)
            settle(dve)
            with dve.Fori(0, NTB // 2) as b:
                chain.enter(b, 16)
                for half in range(2):
                    for j in range(BLK_U):
                        jj = half * BLK_U + j
                        for s in range(2 * j, 2 * j + 2):
                            e = half * 8 + s
                            at = ds(b * (2 * TB) + (half * TB + 4 * s), 4)
                            four = lambda x: x.unsqueeze(2).to_broadcast([P, 4, P])
                            io = iota[:].unsqueeze(1).to_broadcast([P, 4, P])
                            if e < 2:
                                dve.wait_ge(gmm_done, 1 + l * (8 * NTB) + b * 16)
                            else:
                                dve.wait_ge(gmm_done, 1 + l * (8 * NTB) + b * 16 + (e - 1))
                            chain.link(nc.vector.tensor_tensor(hot1[:, e % 2], four(sel1T[:, at]), io, ALU.is_equal))
                            nc.vector.tensor_tensor(hot2[:, e % 2], four(sel2T[:, at]), io, ALU.is_equal)
                            nc.vector.tensor_tensor(hotg[:, e % 2, 0], hot1[:, e % 2],
                                                    four(gThl[:, 0, at].bitcast(F32)), ALU.mult)
                            nc.vector.tensor_tensor(hotg[:, e % 2, 1], hot1[:, e % 2],
                                                    four(gThl[:, 1, at].bitcast(F32)), ALU.mult).then_inc(hot_ready, 1)
                        split_lo(dve, l, M_G + jj + LEAD, b * (2 * BLK_U))
            chain.leave(NTB // 2)
            experts(M_R2, REST // 4)
            def sum_panels(i, last=False):
                for j in range(8):
                    dve.wait_ge(gt_in[j // 4], l * (2 * P) + i * 16 + 16)
                    dve.wait_ge(hin_in[j % 4], l * (4 * P) + i * 32 + 16 * (j // 4 + 1))
                    chain.link(nc.vector.tensor_tensor(
                        wgt[:, j % 2].rearrange("p (b t) -> p b t", t=TB),
                        hin[:, j % 4].rearrange("p (b t) -> p b t", t=TB), gt[:, j // 4, :, j % 4], ALU.mult))
                    dve.wait_ge(gemm_done, 1 + l * M_ALL + i * 8 + (M_V + j - 1))
                    chain.link(nc.vector.tensor_copy(wgthl[:, j % 2, 0], wgt[:, j % 2]))
                    nc.vector.tensor_tensor(wgthl[:, j % 2, 1], wgt[:, j % 2], wgthl[:, j % 2, 0].bitcast(F32),
                                            ALU.subtract).then_inc(w_ready, 1)
                    if not last or j < 8 - LEAD:
                        split_lo(dve, l, M_V + j + LEAD, i * 8)
                    if j == 4:
                        dve.wait_ge(modv_in, l * (16 * MOD_FIRST) + i * 16 + 16)
                        settle(dve)
                        mod_column(mcol[:], modv[:], modv_done)
                        dve.wait_ge(modv_done, l * MOD_FIRST + i + 1)
                        chain.link(nc.vector.tensor_copy(mod[:, ds(i, 1)], mcol[:]))

            settle(dve)
            with dve.Fori(0, P // 8 - 1) as i:
                chain.enter(i, 17)
                sum_panels(i)
            chain.leave(P // 8 - 1)
            sum_panels(P // 8 - 1, last=True)
            for c in range(KC):
                dve.wait_ge(v_done, l * KC + c + 1)
                nc.vector.scalar_tensor_tensor(x_sb[:, c], ps[:, c], mod[:, 5 * KC + c:5 * KC + c + 1], x_sb[:, c],
                                               ALU.mult, ALU.add).then_inc(x_added, 1)
            if dve_chain:
                assert chain.n == dve_chain, chain.n
            else:
                print("dve chain", chain.n)
        rstd(dve, DEPTH, 0)
        dve.wait_ge(rstd_ready, DEPTH * 4 + 1)
        for c in range(KC):
            nc.vector.scalar_tensor_tensor(x_sb[:, c], x_sb[:, c], fin[:, c:c + 1], root[:], ALU.mult, ALU.mult
                                           ).then_inc(out_ready, 1)

    block.__exit__(None, None, None)


def _constants():
    freq = (1.0 / (10000.0 ** (np.arange(0, ROPE, 2, dtype=np.float32) / ROPE))).astype(np.float32)
    s, t = np.arange(P)[:, None], np.arange(P)[None, :]
    band = np.zeros((P, 12, P), np.float32)
    for g, w in enumerate(WINDOWS):
        near = (s <= t) & (s > t - w)
        band[:, g] = near / np.float32(w) - (s == t)
        band[:, 4 + g] = (s > t + P - w) / np.float32(w)
        band[:, 8 + g] = near / np.minimum(t + 1, w).astype(np.float32) - (s == t)
    return np.ascontiguousarray(np.broadcast_to(freq, (P, HALF))), band


def _panels(w):
    l, r, c = w.shape
    return np.ascontiguousarray(w.reshape(l, r // P, P, c // P, P).transpose(0, 3, 2, 1, 4)).reshape(l * (c // P), P, r)


def _columns(v):
    return np.ascontiguousarray(np.swapaxes(v.reshape(v.shape[:-1] + (v.shape[-1] // P, P)), -1, -2))


def _rows(w):
    l, r, c = w.shape
    return np.ascontiguousarray(w.reshape(l, r // P, P, c).transpose(0, 2, 1, 3)).reshape(l, P, -1)


def kernel(**inputs):
    from concourse import bacc
    from concourse.bass_utils import run_bass_kernel_spmd

    a = {k: np.asarray(v) for k, v in inputs.items()}
    L = DEPTH
    freq, band = _constants()
    w = a["w_in"]
    at = np.cumsum([0, 256, 256, Q_LORA, KV_LORA, ROPE, 256, 3 * D])
    zu, zv, cq, ckv, kr, zp, zg = (w[:, :, at[i]:at[i + 1]] for i in range(7))
    zg = zg.reshape(L, D, 3, KC, P).transpose(0, 1, 3, 2, 4).reshape(L, D, 3 * D)
    w_in = np.concatenate([cq, ckv, kr, np.zeros((L, D, P - ROPE), w.dtype), zv, zu, zp, zg], axis=2)
    host = {
        "xT": np.ascontiguousarray(a["x"][0].T.reshape(KC, P, S).transpose(1, 0, 2)),
        "c": a["c"],
        "pos": np.ascontiguousarray(a["positions"][0].reshape(TT, P).T),
        "freq": freq,
        "bands": band,
        "w_mod": np.concatenate([a["w_mod"].transpose(0, 2, 1).reshape(L * N_MOD, P, D),
                                 np.zeros((MOD_FIRST, P, D), w.dtype)]),
        "b_mod": _columns(a["b_mod"]),
        "w_in": _panels(w_in),
        "w_sT": np.ascontiguousarray(a["w_s"].transpose(0, 3, 1, 2)).reshape(L, P, -1),
        "b_s": a["b_s"].reshape(L, -1),
        "qkv_gain": np.concatenate([_columns(a["q_norm"]), _columns(a["kv_norm"])], axis=2),
        "w_uq": _rows(a["w_uq"]),
        "w_ukv": _rows(a["w_ukv"]),
        "w_pool": np.ascontiguousarray(a["w_pool"].reshape(L, 2, 2, 64, 64).transpose(0, 2, 3, 1, 4)).reshape(L, P, -1),
        "pool_scale": _columns(a["pool_scale"]),
        "w_abc": _panels(np.concatenate([a["w_a"], a["w_b"], a["w_c"]], axis=1)),
        "w_o": _panels(a["w_o"]),
        "w_pq": _panels(a["w_pq"]),
        "keysT": np.ascontiguousarray(a["sub_keys"].transpose(0, 4, 1, 2, 3)).reshape(L, P, -1),
        "uT_tab": np.ascontiguousarray(a["u_tab"].reshape(L, P, P, KC, P).transpose(0, 1, 4, 3, 2)).reshape(L * P, P, D),
        "v_tab": a["v_tab"].reshape(L * P, P, D),
        "fin_gain": _columns(a["final_norm"]),
    }
    nc = bacc.Bacc("TRN2", target_bir_lowering=False, num_devices=1)
    args = {k: nc.dram_tensor(f"in_{k}", v.shape, mybir.dt.from_np(v.dtype), kind="ExternalInput").ap()
            for k, v in host.items()}
    args["out"] = nc.dram_tensor("out_x", (P, KC, S), F32, kind="ExternalOutput").ap()
    build_trunk(nc, dve_chain=DVE_CHAIN, **args)
    r = run_bass_kernel_spmd(nc, [{f"in_{k}": v for k, v in host.items()}], core_ids=[0])
    got = r.results[0]["out_x"]
    return np.ascontiguousarray(got.transpose(1, 0, 2).reshape(D, S).T)[None]
```

```python
from concourse import bass, mybir
from concourse.alu_op_type import AluOpType as ALU
import numpy as np

ACT = mybir.ActivationFunctionType
AX = mybir.AxisListType.X
F32 = mybir.dt.float32
F32R = mybir.dt.float32r
I32 = mybir.dt.int32
U32 = mybir.dt.uint32
ds = bass.ds

P = 128
DEPTH = 2
D = 1024
KC = D // P
S = 512
TT = S // P
EPS = 1e-6
HEADS, NOPE, ROPE, VD = 8, 64, 32, 64
QK = NOPE + ROPE
HALF = ROPE // 2
Q_LORA, KV_LORA = 384, 256
WINDOWS = (2, 4, 8, 16)
SCALE = 1.0 / float(np.sqrt(QK))
NEG = -3.0e38
PH, TOPK, NKEYS = 8, 16, 128
TB = 32
NTB = S // TB
AG = 4

N_MOD = 6 * KC
MOD_FIRST = 2 * KC
N_MODX = N_MOD - MOD_FIRST
N_IN = 36
P_KR, P_ZV, P_ZU, P_ZP, P_GATE = 5, 6, 8, 10, 12
FLIPPED = (P_KR, P_ZV, P_ZV + 1, P_ZP, P_ZP + 1)
N_FLIP = len(FLIPPED)
T_U = 6
N_T = PH * (2 + T_U)
REST = 8
BLK_U = 4
M_ABC = N_IN
M_WO = M_ABC + KC
M_T = M_WO + KC
M_R1 = M_T + N_T
M_G = M_R1 + REST
M_R2 = M_G + NTB * BLK_U
M_V = M_R2 + REST
M_ALL = M_V + P
A_R1 = PH * T_U
A_G = A_R1 + REST
A_R2 = A_G + NTB * BLK_U
N_BANKED = M_V // 2
RAW, RING = 4, 4
LEAD = 2


def order_of_panels():
    order = []
    for p in range(N_IN):
        order.append(("m", p))
        if p < N_MODX:
            order.append(("mod", MOD_FIRST + p))
    order += [("m", m) for m in range(M_ABC, M_T)]
    return order


ORDER = order_of_panels()
N_HEAD = len(ORDER)
RAW_ALL = N_HEAD + M_ALL - M_T
assert RAW_ALL % RAW == 0 and N_HEAD % RAW == 0 and M_T % RING == 0 and M_ALL % RING == 0
RAW_USES = RAW_ALL // RAW
RAW_OF = {what: n for n, what in enumerate(ORDER)}


def mixer_steps():
    steps = []
    for p in range(8):
        steps.append(("panel", p))
        if p - 1 in FLIPPED:
            steps.append(("flip", FLIPPED.index(p - 1)))
        if 1 <= p <= 5:
            steps.append(("ssq", p - 1))
        if p == 3:
            steps.append(("root", 0))
        if p == 5:
            steps.append(("root", 1))
    for r in range(2 * TT):
        steps.append(("proj", r))
        if r:
            steps.append(("turn", r - 1))
        steps.append(("panel", 8 + r))
        if 7 + r in FLIPPED:
            steps.append(("flip", FLIPPED.index(7 + r)))
        if r == 3:
            steps.append(("ln", 0))
    steps.append(("turn", 2 * TT - 1))
    steps.append(("panel", 8 + 2 * TT))
    p = 9 + 2 * TT
    for two in ((("ya", 0), ("ya", 1)), (("ya", 2), ("ya", 3)), (("win", 0), ("win", 1)),
                (("pool", 0), ("pool", 1)), (("win", 2), ("win", 3)), (("pool", 2), ("pool", 3))):
        steps += list(two)
        if p < 22:
            steps.append(("panel", p))
            p += 1
    units = HEADS * TT
    rounded = 0
    for u in range(units + 2):
        if u < units:
            steps += [("qk", u), ("norm", u)]
        if 1 <= u <= units:
            steps.append(("pt", u - 1))
        if u >= 2:
            steps.append(("pv", u - 2))
        if p < N_IN:
            steps.append((("half", "panel")[u % 2], p))
            p += u % 2
        else:
            for _ in range(2 if u == units else 1):
                steps.append(("y", rounded))
                rounded += 1
    steps.append(("y", rounded))
    assert p == N_IN and rounded == KC - 1
    return steps


Y_ORDER = (0, 1, 6, 7, 2, 3, 4, 5)


STEPS = mixer_steps()
HALVED = {i for kind, i in STEPS if kind == "half"}


class Chain:

    def __init__(self, eng, sem, per_layer):
        self.eng, self.sem, self.per_layer = eng, sem, per_layer
        self.layer, self.base, self.n = 0, 0, 0

    def start(self, layer):
        self.layer, self.base, self.n = layer * self.per_layer, 0, 0

    def mark(self, ins):
        ins.then_inc(self.sem, 1)
        self.n += 1

    def wait(self):
        self.eng.wait_ge(self.sem, self.layer + self.base + self.n)

    def link(self, ins):
        self.mark(ins)
        self.wait()

    def enter(self, i, count):
        self.outer, self.inner, self.count = self.base, self.n, count
        self.base, self.n = i * count + (self.base + self.n), 0

    def leave(self, times):
        assert self.n == self.count, (self.n, self.count)
        self.base, self.n = self.outer, self.inner + times * self.count


DVE_CHAIN = 536


def build_trunk(nc, xT, c, pos, freq, bands, w_mod, b_mod, w_in, w_sT, b_s, qkv_gain, w_uq, w_ukv,
                w_pool, pool_scale, w_abc, w_o, w_pq, keysT, uT_tab, v_tab, fin_gain, out, dve_chain):
    gate_d = nc.dram_tensor("gate_spill", [3 * KC, P, S], F32, kind="Internal").ap()
    h_d = nc.dram_tensor("expert_spill", [P, P, S], F32, kind="Internal").ap()
    g_d = nc.dram_tensor("weight_spill", [P // AG, P, NTB, AG * TB], F32, kind="Internal").ap()

    top_of = [nc.sbuf_base + -nc.sbuf_base % 32]

    def sb(name, shape, dt=F32, at=None):
        size = 4 * int(np.prod(shape[1:]))
        size += -size % 32
        off = top_of[0] if at is None else at
        if at is None:
            top_of[0] += size
        return nc.alloc_sbuf_tensor_at(name, shape, dt, offset=off)

    x_sb = sb("x_sb", [P, KC, S])
    mov = sb("mov", [P, 2, KC, S], F32R)
    raw = sb("raw", [P, RAW, KC, P])
    whl = sb("whl", [P, RING, 2, KC, P], F32R)
    mod = sb("mod_cols", [P, N_MOD])
    bmod = sb("bmod", [P, N_MOD])
    c_act = sb("c_act", [P, D])
    fin = sb("fin", [P, KC])
    ident = sb("ident", [P, P])
    ones = sb("ones", [P, P])
    causal = sb("causal", [P, P])
    iota = sb("iota", [P, P])
    eps = sb("eps", [P, 1])
    cos = sb("cos", [P, TT, HALF])
    sin = sb("sin", [P, TT, HALF])
    gain = sb("gain", [P, 5])
    pscale = sb("pscale", [P, 2])
    bn6 = sb("bn6", [P, TT, 6])
    bn2 = sb("bn2", [P, TT, 2])
    lnr = sb("lnr", [P, TT])
    mcol = sb("mcol", [P, 1])
    mx = sb("mx", [P, 2])
    nmx = sb("nmx", [P, 2])
    rsum = sb("rsum", [P, 2])
    rinv = sb("rinv", [P, 2])
    sq = sb("sq", [P, 2, S])
    root = sb("root", [P, S])
    free = top_of[0]

    qT = sb("qT", [P, HEADS, S])
    kT = sb("kT", [P, HEADS, S])
    mrg = sb("mrg", [P, 2, KC, S], F32R, at=free)
    vh = sb("vh", [P, TT, HEADS * VD])
    y_at = top_of[0]
    y = sb("y", [P, KC, S])
    ukv = sb("ukv", [P, 2, HEADS * (NOPE + VD)], at=y_at)
    tok = sb("tok", [P, 2, HEADS, QK], at=y_at + 8192)
    lat_at = top_of[0]
    lat = sb("lat", [P, 5, S])
    wsT = sb("wsT", [P, 4, P], at=lat_at)
    bsb = sb("bsb", [P, 4, P], at=lat_at + 2048)
    band = sb("band", [P, 12, P], at=lat_at + 4096)
    gst_at = top_of[0]
    gst = sb("gst", [P, 6, S])
    uq = sb("uq", [P, 3, HEADS * QK], at=gst_at)
    kr = sb("kr", [P, TT, ROPE])
    rt = sb("rt", [P, 4, HEADS, HALF])
    ug = sb("ug", [P, 2, S])
    pv_at = top_of[0]
    vg = sb("vg", [P, TT, 2 * P])
    zp = sb("zp", [P, TT, 2 * P])
    pr = sb("pr", [P, 2, S], at=pv_at)
    prT = sb("prT", [P, 2, S], at=pv_at + 4096)
    wpl = sb("wpl", [P, 2, 64])
    ht_at = top_of[0]
    ytmp = sb("ytmp", [P, 2, S])
    ht = sb("ht", [P, 2, S], at=ht_at)
    assert top_of[0] <= nc.sbuf_usable_end, top_of[0]

    top_of[0] = free
    hst = sb("hst", [P, 2, S])
    topv = sb("topv", [P, TT, PH, TOPK])
    sel1 = sb("sel1", [P, TT, PH, TOPK])
    sel2 = sb("sel2", [P, TT, PH, TOPK])
    den = sb("den", [P, TT * PH])
    dinv = sb("dinv", [P, TT * PH])
    sel1T = sb("sel1T", [P, S])
    sel2T = sb("sel2T", [P, S])
    gT = sb("gT", [P, S])
    gThl = sb("gThl", [P, 2, S], F32R)
    pick_at = top_of[0]
    qh = sb("qh", [P, 2, S])
    keys = sb("keys", [P, 2 * PH, P])
    sc2 = sb("sc2", [P, TT, P])
    v12 = sb("v12", [P, TT, 2, TOPK])
    i12u = sb("i12u", [P, TT, 2, TOPK], U32)
    i12 = sb("i12", [P, TT, 2, TOPK])
    cand = sb("cand", [P, TT, TOPK * TOPK])
    cand2 = sb("cand2", [P, TT, TOPK * TOPK])
    topc = sb("topc", [P, TT, TOPK])
    posu = sb("posu", [P, TT, TOPK], U32)
    abu = sb("abu", [P, 2, TT, TOPK], U32)
    abf = sb("abf", [P, 2, TT, TOPK])
    eq = sb("eq", [P, TT, TOPK, TOPK])
    assert top_of[0] <= nc.sbuf_usable_end
    top_of[0] = pick_at
    stage = sb("stage", [P, 2, P, TB])
    hot2 = sb("hot2", [P, 2, 4, P], F32R)
    hot1 = sb("hot1", [P, 2, 4, P])
    hotg = sb("hotg", [P, 2, 2, 4, P], F32R)
    low = sb("low", [P, 2, 4, P])
    assert top_of[0] <= nc.sbuf_usable_end
    gt = sb("gt", [P, 2, NTB, AG, TB], at=pick_at)
    top_of[0] = pick_at + 2 * 4 * NTB * AG * TB
    hin = sb("hin", [P, 4, S])
    wgt = sb("wgt", [P, 2, S])
    wgthl = sb("wgthl", [P, 2, 2, S], F32R)
    assert top_of[0] <= nc.sbuf_usable_end
    pos_i = sb("pos_i", [P, TT], I32, at=free)
    pos_f = sb("pos_f", [P, TT], at=free + 32)
    frq = sb("frq", [P, HALF], at=free + 64)
    ang = sb("ang", [P, TT, HALF], at=free + 256)
    turns = sb("turns", [P, TT, HALF], at=free + 512)
    over = sb("over", [P, TT, HALF], at=free + 768)
    c_sig = sb("c_sig", [P, D], at=free + 2048)
    mod0 = sb("mod0", [P, 4, D], at=free + 4 * D + 2048)
    assert free + 4 * D + 2048 + 16 * D <= lat_at
    modv = sb("modv", [P, D], at=free)

    ps = nc.alloc_psum_tensor("ps", [P, 8, S], F32)
    sem = nc.alloc_semaphore

    raw_in = [sem(f"raw_in{i}") for i in range(RAW)]
    hi_done, lo_done, gemm_done = sem("hi_done"), sem("lo_done"), sem("gemm_done")
    mod_done, mod0_done, modv_done, modv_in = sem("mod_done"), sem("mod0_done"), sem("modv_done"), sem("modv_in")
    mod0_in = [sem(f"mod0_in{i}") for i in range(4)]
    bank_free = [sem("bank0_free"), sem("bank1_free")]
    c_in, x_in = sem("c_in"), sem("x_in")
    start_in, consts_made, rope_made = sem("start_in"), sem("consts_made"), sem("rope_made")
    c_ready = sem("c_ready")
    bias_in, params_in, mid_in, keys_in = sem("bias_in"), sem("params_in"), sem("mid_in"), sem("keys_in")
    ws_masked = sem("ws_masked")
    sq_ready, sq_used = sem("sq_ready"), sem("sq_used")
    root_ready, rstd_ready = sem("root_ready"), sem("rstd_ready")
    t_ready, t_hi, mov_ready = sem("t_ready"), sem("t_hi"), sem("mov_ready")
    lat_norm = sem("lat_norm")
    flipped, flip_used = sem("flipped"), sem("flip_used")
    ln_var, ln_root, ln_ready = sem("ln_var"), sem("ln_root"), sem("ln_ready")
    proj_ready, tok_act, tok_dve = sem("proj_ready"), sem("tok_act"), sem("tok_dve")
    turn_ready, turn_act, turn_dve = sem("turn_ready"), sem("turn_act"), sem("turn_dve")
    side_ready, side_out = sem("side_ready"), sem("side_out")
    qk_ready, max_ready, exp_ready, prob_ready = (
        sem("qk_ready"), sem("max_ready"), sem("exp_ready"), sem("prob_ready"))
    pt_ready, prT_ready, pv_ready, y_ready = sem("pt_ready"), sem("prT_ready"), sem("pv_ready"), sem("y_ready")
    y_hi = sem("y_hi")
    gate_out = [sem(f"gate_out{i}") for i in range(6)]
    gate_in = [sem(f"gate_in{i}") for i in range(6)]
    merged, merged_hi, merged_lo = sem("merged"), sem("merged_hi"), sem("merged_lo")
    score_ready, score_used = sem("score_ready"), sem("score_used")
    h_out = [sem("h_out0"), sem("h_out1")]
    g_sub, g_exp, g_norm = sem("g_sub"), sem("g_exp"), sem("g_norm")
    sel_turned, sel_act, sel_dve = sem("sel_turned"), sem("sel_act"), sem("sel_dve")
    low_ready = sem("low_ready")
    hot1_ready, hot_lo_ready = sem("hot1_ready"), sem("hot_lo_ready")
    hot_ready, gmm_done, stage_ready = sem("hot_ready"), sem("gmm_done"), sem("stage_ready")
    stage_out = [sem("stage_out0"), sem("stage_out1")]
    gt_in = [sem("gt_in0"), sem("gt_in1")]
    hin_in = [sem(f"hin_in{i}") for i in range(4)]
    w_ready = sem("w_ready")
    v_done, x_added = sem("v_done"), sem("x_added")
    out_ready, out_done = sem("out_ready"), sem("out_done")
    dve_step, setup_step = sem("dve_step"), sem("setup_step")

    def raw_n(m):
        return RAW_OF[("m", m)] if m < M_T else N_HEAD + m - M_T

    def wait_raw(eng, l, m, more=0):
        n = raw_n(m)
        eng.wait_ge(raw_in[n % RAW], l * (16 * RAW_USES) + more * (16 // RAW) + 16 * (n // RAW + 1))

    def split_hi(act, l, m, more=0):
        wait_raw(act, l, m, more)
        act.wait_ge(gemm_done, 1 + l * M_ALL + more + max(m - RING + 1, 0))
        nc.scalar.copy(whl[:, m % RING, 0], raw[:, raw_n(m) % RAW]).then_inc(hi_done, 1)

    def banked(m, l, more_half=0):
        return bank_free[m % 2], 1 + l * N_BANKED + more_half + m // 2 + 1

    def split_lo(dve, l, m, more=0):
        dve.wait_ge(hi_done, l * M_ALL + more + m + 1)
        nc.vector.tensor_tensor(whl[:, m % RING, 1], raw[:, raw_n(m) % RAW],
                                whl[:, m % RING, 0].bitcast(F32), ALU.subtract).then_inc(lo_done, 1)

    def gemm(pe, l, m, src=mov, more=0, more_half=0, rows=None, chunks=range(KC)):
        pe.wait_ge(lo_done, 1 + l * M_ALL + more + m + 1)
        pe.wait_ge(bank_free[m % 2], 1 + l * N_BANKED + more_half + m // 2)
        w = whl[:, m % RING]
        for k in chunks:
            if rows:
                pe.wait_ge(rows[0], rows[1] + k + 1)
            nc.tensor.matmul(ps[:, m % 2], w[:, 0, k], src[:, 0, k], start=(k == 0), stop=False)
            nc.tensor.matmul(ps[:, m % 2], w[:, 0, k], src[:, 1, k], start=False, stop=False)
            mm = nc.tensor.matmul(ps[:, m % 2], w[:, 1, k], src[:, 0, k], start=False, stop=(k == KC - 1))
        if chunks[-1] == KC - 1:
            mm.then_inc(gemm_done, 1)

    def mod_column(column, panel, signal):
        nc.vector.tensor_tensor_reduce(panel, panel, c_act[:], 1.0, 0.0, ALU.mult, ALU.add, column
                                       ).then_inc(signal, 1)

    SQ_H1, SQ_LAT, SQ_H2, SQ_ALL = 0, KC, KC + 5, 2 * KC + 5

    def square(act, l, q, src):
        act.wait_ge(sq_used, 1 + l * SQ_ALL + max(q - 1, 0))
        nc.scalar.activation(sq[:, q % 2], src, ACT.Square).then_inc(sq_ready, 1)

    def sum_squares(pe, l, q, bank, first, last):
        pe.wait_ge(sq_ready, l * SQ_ALL + q + 1)
        mm = nc.tensor.matmul(ps[:, bank], ones[:], sq[:, q % 2], start=first, stop=last)
        mm.then_inc(sq_used, 1)
        return mm

    def rstd(dve, l, k):
        dve.wait_ge(root_ready, l * 4 + k + 1)
        nc.vector.reciprocal(root[:], root[:]).then_inc(rstd_ready, 1)

    SSQ_BANK = (2, 2, 3, 2)

    def take_root(act, l, k, width):
        act.wait_ge(sq_used, 1 + l * SQ_ALL + (SQ_H1 + KC, SQ_LAT + 3, SQ_LAT + 5, SQ_ALL)[k])
        if k == 2:
            act.wait_ge(lat_norm, l * 5 + 3)
        elif k:
            act.wait_ge(mov_ready, l * (3 * KC) + (KC, None, 2 * KC)[k - 1])
        nc.scalar.activation(root[:], ps[:, SSQ_BANK[k]], ACT.Sqrt, bias=eps[:], scale=1.0 / width
                             ).then_inc(root_ready, 1)

    def settle(eng):
        eng.nop(nofuse=True)

    block = nc.Block()
    block.__enter__()

    primed = [gemm_done, lo_done, *bank_free, sq_used, flip_used, tok_act, tok_dve, turn_act, turn_dve, side_out,
              exp_ready, prT_ready, y_ready, pt_ready, score_ready, score_used, stage_ready, gmm_done]

    N_START, N_PARAMS, N_MID = 3, 5, 3

    @block.sync
    def _(sp):
        for signal in primed:
            sp.sem_inc(signal, 1)

        def load(l, n, src, freed=None):
            slot = n % RAW
            if freed is None:
                if n < RAW:
                    sp.wait_ge(lo_done, 1 + l * M_ALL)
                else:
                    kind, i = ORDER[n - RAW]
                    if kind == "mod":
                        sp.wait_ge(mod_done, l * N_MODX + i - MOD_FIRST + 1)
                    else:
                        sp.wait_ge(lo_done, 1 + l * M_ALL + i + 1)
            sp.dma_start(raw[:, slot], src).then_inc(raw_in[slot], 16)

        def panel(table, at):
            return table[ds(at, 1)].rearrange("o p (k c) -> p (o k) c", k=KC)

        for i in range(MOD_FIRST):
            if i >= 4:
                sp.wait_ge(mod0_done, i - 3)
            sp.dma_start(mod0[:, i % 4], w_mod[i]).then_inc(mod0_in[i % 4], 16)
            if i == 3:
                sp.wait_ge(x_in, 16)
                sp.sem_inc(x_added, KC)
        with sp.Fori(0, DEPTH) as l:
            for n, (kind, i) in enumerate(ORDER):
                if kind == "mod":
                    src = w_mod[ds(l * N_MOD + i, 1)].rearrange("o p (k c) -> p (o k) c", k=KC)
                elif i < M_ABC:
                    src = panel(w_in, l * N_IN + i)
                elif i < M_WO:
                    src = panel(w_abc, l * KC + (i - M_ABC))
                else:
                    src = panel(w_o, l * KC + (i - M_WO))
                load(l, n, src)
            settle(sp)
            with sp.Fori(0, PH) as h:
                for j in range(2 + T_U):
                    src = panel(w_pq, l * 2 * PH + h * 2 + j) if j < 2 else \
                        panel(uT_tab, l * P + h * T_U + (j - 2))
                    sp.wait_ge(lo_done, 1 + l * M_ALL + h * (2 + T_U) + (M_T + j - RAW + 1))
                    load(l, N_HEAD + j, src, freed=True)

            def run(first_m, first_a, times, table):
                settle(sp)
                with sp.Fori(0, times) as i:
                    for j in range(4):
                        sp.wait_ge(lo_done, 1 + l * M_ALL + i * 4 + (first_m + j - RAW + 1))
                        load(l, raw_n(first_m + j), panel(table, l * P + i * 4 + (first_a + j)), freed=True)

            run(M_R1, A_R1, (M_V - M_R1) // 4, uT_tab)
            run(M_V, 0, P // 4, v_tab)
        for c in range(KC):
            sp.wait_ge(out_ready, c + 1)
            sp.dma_start(out[:, c], x_sb[:, c]).then_inc(out_done, 16)
        sp.wait_ge(out_done, 16 * KC)

    @block.gpsimd
    def _(pool):
        pool.dma_start(c_act[:], c.to_broadcast([P, D])).then_inc(c_in, 16)
        pool.dma_start(pos_i[:], pos).then_inc(start_in, 16)
        pool.dma_start(frq[:], freq).then_inc(start_in, 16)
        pool.dma_start(fin[:], fin_gain).then_inc(start_in, 16)
        pool.dma_start(x_sb[:], xT).then_inc(x_in, 16)
        nc.gpsimd.memset(ones[:], 1.0)
        nc.gpsimd.memset(eps[:], EPS)
        nc.gpsimd.memset(causal[:], 0.0)
        nc.gpsimd.memset(ident[:], 0.0).then_inc(consts_made, 1)
        pool.wait_ge(consts_made, 1)
        nc.gpsimd.affine_select(out=ident[:], in_=ident[:], compare_op=ALU.not_equal, fill=1.0, base=0,
                                pattern=[[1, P]], channel_multiplier=-1)
        nc.gpsimd.affine_select(out=causal[:], in_=causal[:], compare_op=ALU.is_ge, fill=-1.0e30, base=0,
                                pattern=[[-1, P]], channel_multiplier=1)
        nc.gpsimd.iota(iota[:], [[1, P]], base=0, channel_multiplier=0,
                       allow_small_or_imprecise_dtypes=True).then_inc(consts_made, 1)
        pool.wait_ge(consts_made, 2)
        for half in range(2):
            pool.dma_start(h_d[half, 0:1, :16], ones[0:1, :16]).then_inc(h_out[half], 16)
            pool.dma_start(g_d[half, 0:1, 0, :16], ones[0:1, :16]).then_inc(stage_out[half], 16)
        with pool.Fori(0, DEPTH) as l:
            pool.wait_ge(rope_made, 1)
            one = lambda t: t[ds(l, 1)].rearrange("o p n -> p (o n)")
            pool.dma_start(bmod[:], one(b_mod)).then_inc(bias_in, 16)
            pool.dma_start(gain[:], one(qkv_gain)).then_inc(params_in, 16)
            pool.dma_start(pscale[:], one(pool_scale)).then_inc(params_in, 16)
            pool.dma_start(wpl[:].rearrange("p a b -> p (a b)"), one(w_pool)).then_inc(params_in, 16)
            pool.wait_ge(mov_ready, l * (3 * KC) + 2)
            settle(pool)
            pool.dma_start(uq[:].rearrange("p a b -> p (a b)"), one(w_uq)).then_inc(params_in, 16)
            pool.dma_start(ukv[:].rearrange("p a b -> p (a b)"), one(w_ukv)).then_inc(params_in, 16)
            for j in range(3 * KC):
                if j == 0:
                    pool.wait_ge(proj_ready, l * 2 * TT + 2 * TT)
                    settle(pool)
                    pool.dma_start(wsT[:].rearrange("p a b -> p (a b)"), one(w_sT)).then_inc(mid_in, 16)
                    pool.dma_start(bsb[:].rearrange("p a b -> p (a b)"),
                                   b_s[ds(l, 1)].to_broadcast([P, 4 * P])).then_inc(mid_in, 16)
                    pool.dma_start(band[:], bands).then_inc(mid_in, 16)
                    pool.wait_ge(mid_in, l * (16 * N_MID) + 16 * N_MID)
                    settle(pool)
                    nc.gpsimd.affine_select(out=wsT[:], in_=wsT[:], compare_op=ALU.is_ge, fill=0.0, base=0,
                                            pattern=[[0, 4], [1, P]], channel_multiplier=-1
                                            ).then_inc(ws_masked, 1)
                pool.wait_ge(*banked(P_GATE + j, l))
                settle(pool)
                pool.dma_start(gate_d[j], gst[:, j % 6]).then_inc(gate_out[j % 6], 16)
            for j in range(3 * KC):
                if j < 6:
                    pool.wait_ge(gate_out[j], l * 64 + 64)
                else:
                    pool.wait_ge(merged, l * KC + j // 3 - 1)
                settle(pool)
                pool.dma_start(gst[:, j % 6], gate_d[j]).then_inc(gate_in[j % 6], 16)
            pool.wait_ge(merged, l * KC + KC)
            pool.wait_ge(gemm_done, 1 + l * M_ALL + M_T)
            settle(pool)
            pool.dma_start(keys[:].rearrange("p a b -> p (a b)"), one(keysT)).then_inc(keys_in, 16)

            def store_h(a, more, slot, m, more_m):
                pool.wait_ge(*banked(m, l, more_m))
                settle(pool)
                pool.dma_start(h_d[ds(more + a, 1)].rearrange("o p t -> p (o t)"), hst[:, slot]
                               ).then_inc(h_out[slot], 16)

            settle(pool)
            with pool.Fori(0, PH) as h:
                for j in range(T_U):
                    store_h(j, h * T_U, j % 2, M_T + 2 + j, h * ((2 + T_U) // 2))
            settle(pool)
            with pool.Fori(0, REST // 4) as i:
                for j in range(4):
                    store_h(A_R1 + j, i * 4, j % 2, M_R1 + j, i * 2)
            settle(pool)
            with pool.Fori(0, NTB // 2) as b:
                for half in range(2):
                    for j in range(BLK_U):
                        for s in range(2 * j, 2 * j + 2):
                            e = half * 8 + s
                            at = ds(b * (2 * TB) + (half * TB + 4 * s), 4)
                            pool.wait_ge(hot1_ready, l * (8 * NTB) + b * 16 + e + 1)
                            nc.gpsimd.tensor_tensor(hotg[:, e % 2, 1], hot1[:, e % 2],
                                                    gThl[:, 1, at].bitcast(F32).unsqueeze(2).to_broadcast([P, 4, P]),
                                                    ALU.mult).then_inc(hot_lo_ready, 1)
                        store_h(A_G + half * BLK_U + j, b * (2 * BLK_U), j % 2,
                                M_G + half * BLK_U + j, b * BLK_U)
                    pool.wait_ge(stage_ready, 1 + l * (8 * NTB) + b * 16 + half * 8 + 8)
                    settle(pool)
                    pool.dma_start(
                        g_d[:, :, ds(b * 2 + half, 1)].rearrange("a p o x -> p a (o x)"),
                        stage[:, half].rearrange("p (g a) t -> p g (a t)", a=AG)).then_inc(stage_out[half], 16)

            def load_g(half, block_at):
                settle(pool)
                pool.dma_start(gt[:, half].rearrange("p b a t -> p (b a t)"),
                               g_d[ds(block_at, 1)].rearrange("o p b x -> p (o b x)")).then_inc(gt_in[half], 16)

            def load_h(slot, a):
                settle(pool)
                pool.dma_start(hin[:, slot], h_d[ds(a, 1)].rearrange("o p t -> p (o t)")).then_inc(hin_in[slot], 16)

            def load_mod(i):
                settle(pool)
                pool.dma_start(modv[:], w_mod[ds((l + 1) * N_MOD + i, 1)].rearrange("o p k -> p (o k)")
                               ).then_inc(modv_in, 16)

            first_loads = {3: [("g", 0)], 4: [("g", 1)], 5: [("h", 0), ("h", 1)], 6: [("h", 2), ("h", 3)]}
            for a in range(REST):
                if a == 3:
                    for half in range(2):
                        pool.wait_ge(stage_out[half], 16 + l * (8 * NTB) + 8 * NTB)
                for what, n in first_loads.get(a, []):
                    if what == "g":
                        load_g(n, n)
                    else:
                        pool.wait_ge(h_out[n % 2], 16 + l * (8 * P) + 16 * (n // 2 + 1))
                        load_h(n, n)
                store_h(A_R2 + a, 0, a % 2, M_R2 + a, 0)
            for half in range(2):
                pool.wait_ge(h_out[half], 16 + l * (8 * P) + 8 * P)
            load_mod(0)
            settle(pool)
            with pool.Fori(0, P // 8 - 1) as i:
                for half in range(2):
                    for j in range(4):
                        pool.wait_ge(w_ready, l * P + i * 8 + (half * 4 + j + 1))
                        load_h(j, i * 8 + (half * 4 + j + 4))
                    load_g(half, i * 2 + (half + 2))
                pool.wait_ge(modv_done, l * MOD_FIRST + i + 1)
                load_mod(i + 1)
            for j in range(4):
                pool.wait_ge(w_ready, l * P + (P - 8 + j + 1))
                load_h(j, P - 4 + j)

    @block.tensor
    def _(pe):
        pe.wait_ge(consts_made, 2)
        with pe.Fori(0, DEPTH) as l:
            for q in range(KC):
                if q == 0:
                    pe.wait_ge(x_added, l * KC + 3)
                sum_squares(pe, l, SQ_H1 + q, 2, q == 0, q == KC - 1)
            pe.wait_ge(x_added, l * KC + KC)
            for kind, i in STEPS:
                if kind == "half":
                    gemm(pe, l, i, chunks=range(KC // 2))
                elif kind == "panel" and i in HALVED:
                    gemm(pe, l, i, chunks=range(KC // 2, KC))
                elif kind == "panel":
                    gemm(pe, l, i, rows=(mov_ready, l * 3 * KC) if i == 0 else None)
                elif kind == "flip":
                    pe.wait_ge(*banked(FLIPPED[i], l))
                    pe.wait_ge(flip_used, 1 + l * N_FLIP + i)
                    for t in range(TT):
                        mm = nc.tensor.transpose(ps[:, 7, t * P:(t + 1) * P],
                                                 ytmp[:, i % 2, t * P:(t + 1) * P], ident[:])
                    mm.then_inc(flipped, 1)
                elif kind == "ssq":
                    if i == 0:
                        pe.wait_ge(root_ready, l * 4 + 1)
                    sum_squares(pe, l, SQ_LAT + i, 2 if i < 3 else 3, i in (0, 3), i in (2, 4))
                elif kind == "proj":
                    t = i % TT
                    if i == 0:
                        pe.wait_ge(params_in, l * (16 * N_PARAMS) + 16 * N_PARAMS)
                    pe.wait_ge(lat_norm, l * 5 + (3 if i < TT else 5))
                    pe.wait_ge(tok_act, 1 + l * 2 * TT + i)
                    pe.wait_ge(tok_dve, 1 + l * 2 * TT + i)
                    flat = ps[:, 4:6].rearrange("p b n -> p (b n)")
                    w, ks, first, width = (uq, 3, 0, HEADS * QK) if i < TT else (ukv, 2, 3, HEADS * (NOPE + VD))
                    for c0 in range(0, width, S):
                        c1 = min(c0 + S, width)
                        for k in range(ks):
                            mm = nc.tensor.matmul(flat[:, c0:c1], lat[:, first + k, t * P:(t + 1) * P],
                                                  w[:, k, c0:c1], start=(k == 0), stop=(k == ks - 1))
                    mm.then_inc(proj_ready, 1)
                elif kind == "turn":
                    if i == 0:
                        pe.wait_ge(root_ready, l * 4 + 3)
                    pe.wait_ge(tok_act, 1 + l * 2 * TT + i + 1)
                    pe.wait_ge(tok_dve, 1 + l * 2 * TT + i + 1)
                    pe.wait_ge(turn_act, 1 + l * 2 * TT + i)
                    pe.wait_ge(turn_dve, 1 + l * 2 * TT + i)
                    for h in range(HEADS):
                        mm = nc.tensor.transpose(ps[:QK, 2 + h // 4, (h % 4) * P:(h % 4 + 1) * P],
                                                 tok[:, i % 2, h, :], ident[:])
                    mm.then_inc(turn_ready, 1)
                elif kind == "ya":
                    if i == 0:
                        pe.wait_ge(ws_masked, l + 1)
                        pe.wait_ge(ln_ready, l + 1)
                        pe.wait_ge(tok_act, 1 + l * 2 * TT + 2 * TT)
                        pe.wait_ge(tok_dve, 1 + l * 2 * TT + 2 * TT)
                    pe.wait_ge(side_out, 1 + l * 12 + max(i - 1, 0))
                    for n in range(TT):
                        mm = nc.tensor.matmul(ps[:, 4 + i % 2, n * P:(n + 1) * P],
                                              vg[:, n, (i // 2) * P:(i // 2 + 1) * P], wsT[:, i],
                                              start=True, stop=True)
                    mm.then_inc(side_ready, 1)
                elif kind == "win":
                    if i == 0:
                        pe.wait_ge(flip_used, 1 + l * N_FLIP + N_FLIP)
                    e = 4 + (i if i < 2 else i + 2)
                    pe.wait_ge(side_out, 1 + l * 12 + e - 1)
                    r0 = 64 * (i % 2)
                    for n in range(TT):
                        o = ps[r0:r0 + 64, 4 + i % 2, n * P:(n + 1) * P]
                        mm = nc.tensor.matmul(o, zp[:, n, i * 64:(i + 1) * 64], band[:, i if n else 8 + i],
                                              start=True, stop=(n == 0))
                        if n:
                            mm = nc.tensor.matmul(o, zp[:, n - 1, i * 64:(i + 1) * 64], band[:, 4 + i],
                                                  start=False, stop=True)
                    mm.then_inc(side_ready, 1)
                elif kind == "pool":
                    e = 6 + (i if i < 2 else i + 2)
                    pe.wait_ge(side_out, 1 + l * 12 + e - 1)
                    r0 = 64 * (i % 2)
                    settle(pe)
                    mm = nc.tensor.matmul(ps[r0:r0 + 64, 4 + i % 2], wpl[r0:r0 + 64, i // 2],
                                          ytmp[r0:r0 + 64, i % 2], start=True, stop=True)
                    mm.then_inc(side_ready, 1)
                elif kind == "qk":
                    h, t = divmod(i, TT)
                    if i == 0:
                        pe.wait_ge(turn_act, 1 + l * 2 * TT + 2 * TT)
                        pe.wait_ge(turn_dve, 1 + l * 2 * TT + 2 * TT)
                    pe.wait_ge(exp_ready, 1 + l * 32 + max(i - 1, 0))
                    n = (t + 1) * P
                    nc.tensor.matmul(ps[:, 2 + i % 2, :n], qT[:QK, h, t * P:n], kT[:QK, h, :n],
                                     start=True, stop=False)
                    nc.tensor.matmul(ps[:, 2 + i % 2, t * P:n], ident[:], causal[:],
                                     start=False, stop=True).then_inc(qk_ready, 1)
                elif kind == "pt":
                    t = i % TT
                    pe.wait_ge(prob_ready, l * 32 + i + 1)
                    pe.wait_ge(side_out, 1 + l * 12 + 12)
                    pe.wait_ge(prT_ready, 1 + l * 32 + max(i - 1, 0))
                    for j in range(t + 1):
                        mm = nc.tensor.transpose(ps[:, 4 + i % 2, j * P:(j + 1) * P],
                                                 pr[:, i % 2, j * P:(j + 1) * P], ident[:])
                    mm.then_inc(pt_ready, 1)
                elif kind == "pv":
                    h, t = divmod(i, TT)
                    r0 = 64 * (h % 2)
                    pe.wait_ge(prT_ready, 1 + l * 32 + i + 1)
                    if t == 0:
                        pe.wait_ge(y_ready, 1 + l * HEADS + max(h - 1, 0))
                    for j in range(t + 1):
                        mm = nc.tensor.matmul(ps[r0:r0 + 64, 6, t * P:(t + 1) * P],
                                              vh[:, j, h * VD:(h + 1) * VD], prT[:, i % 2, j * P:(j + 1) * P],
                                              start=(j == 0), stop=(j == t))
                    mm.then_inc(pv_ready, 1)
            pe.wait_ge(y_ready, 1 + l * HEADS + HEADS)
            pe.wait_ge(prT_ready, 1 + l * 32 + 32)
            pe.wait_ge(exp_ready, 1 + l * 32 + 32)
            for i in range(KC):
                m = M_ABC + i
                pe.wait_ge(lo_done, 1 + l * M_ALL + m + 1)
                pe.wait_ge(bank_free[m % 2], 1 + l * N_BANKED + m // 2)
                w = whl[:, m % RING]
                for n, k in enumerate(Y_ORDER):
                    if i == 0:
                        pe.wait_ge(mov_ready, l * 3 * KC + KC + n + 1)
                    b = (0, 0, 1, 1, 1, 1, 2, 2)[k]
                    first, last = k in (0, 2, 6), k in (1, 5, 7)
                    o = ps[:, (m % 2, 2 + m % 2, 4 + m % 2)[b]]
                    nc.tensor.matmul(o, w[:, 0, k], mov[:, 0, k], start=first, stop=False)
                    nc.tensor.matmul(o, w[:, 0, k], mov[:, 1, k], start=False, stop=False)
                    mm = nc.tensor.matmul(o, w[:, 1, k], mov[:, 0, k], start=False, stop=last)
                mm.then_inc(gemm_done, 1)
            for i in range(KC):
                gemm(pe, l, M_WO + i, src=mrg, rows=(merged_lo, l * KC) if i == 0 else None)
                if i == 1:
                    pe.wait_ge(merged, l * KC + KC)
                if i:
                    sum_squares(pe, l, SQ_H2 + i - 1, 2, i == 1, False)
            sum_squares(pe, l, SQ_H2 + KC - 1, 2, False, True)
            settle(pe)
            with pe.Fori(0, PH) as h:
                for j in range(2 + T_U):
                    m = M_T + j
                    gemm(pe, l, m, more=h * (2 + T_U), more_half=h * ((2 + T_U) // 2),
                         rows=None if j else (mov_ready, l * 3 * KC + 2 * KC))
                    if j in (2, 3):
                        side = j - 2
                        if side == 0:
                            pe.wait_ge(keys_in, l * 16 + 16)
                        pe.wait_ge(*banked(M_T + side, l, h * ((2 + T_U) // 2)))
                        pe.wait_ge(score_used, 1 + l * 2 * PH + h * 2 + side)
                        for t in range(TT):
                            mm = nc.tensor.matmul(ps[:, 2 + side, t * P:(t + 1) * P],
                                                  qh[:, side, t * P:(t + 1) * P],
                                                  keys[:, ds(h * 2 + side, 1)].rearrange("p o k -> p (o k)"),
                                                  start=True, stop=True)
                        mm.then_inc(score_ready, 1)

            def experts(first_m, times):
                settle(pe)
                with pe.Fori(0, times) as i:
                    for j in range(4):
                        gemm(pe, l, first_m + j, more=i * 4, more_half=i * 2)

            experts(M_R1, REST // 4)
            pe.wait_ge(score_used, 1 + l * 2 * PH + 2 * PH)
            pe.wait_ge(g_norm, l + 1)
            for b, src in ((2, sel1), (3, sel2), (4, topv)):
                for t in range(TT):
                    mm = nc.tensor.transpose(ps[:, b, t * P:(t + 1) * P],
                                             src[:, t].rearrange("p h k -> p (h k)"), ident[:])
            mm.then_inc(sel_turned, 1)
            pe.wait_ge(sel_dve, l + 1)
            settle(pe)
            with pe.Fori(0, NTB // 2) as b:
                for half in range(2):
                    for j in range(BLK_U):
                        jj = half * BLK_U + j
                        gemm(pe, l, M_G + jj, more=b * (2 * BLK_U), more_half=b * BLK_U)
                        for s in range(2 * j, 2 * j + 2):
                            e = half * 8 + s
                            pe.wait_ge(hot_ready, l * (8 * NTB) + b * 16 + e + 1)
                            pe.wait_ge(hot_lo_ready, l * (8 * NTB) + b * 16 + e + 1)
                            bank = 4 + 2 * (e % 2)
                            for t in range(4):
                                mm = nc.tensor.matmul(ps[:, bank + t // 2, t % 2 * 2 * P:(t % 2 + 1) * 2 * P],
                                                      hot2[:, e % 2, t], hotg[:, e % 2, :, t], start=True, stop=True)
                            mm.then_inc(gmm_done, 1)
            experts(M_R2, REST // 4)
            pe.wait_ge(bank_free[0], 1 + l * N_BANKED + N_BANKED)
            pe.wait_ge(bank_free[1], 1 + l * N_BANKED + N_BANKED)
            pe.wait_ge(sel_act, l + 1)
            pe.wait_ge(stage_ready, 1 + l * (8 * NTB) + 8 * NTB)

            def sum_panels(at, first=False, last=False):
                for j in range(4):
                    pe.wait_ge(lo_done, 1 + l * M_ALL + at + (M_V + j + 1))
                    pe.wait_ge(w_ready, l * P + at + (j + 1))
                    w = whl[:, (M_V + j) % RING]
                    for c in range(KC):
                        nc.tensor.matmul(ps[:, c], w[:, 0, c], wgthl[:, j % 2, 0], start=first and j == 0, stop=False)
                        nc.tensor.matmul(ps[:, c], w[:, 0, c], wgthl[:, j % 2, 1], start=False, stop=False)
                        mm = nc.tensor.matmul(ps[:, c], w[:, 1, c], wgthl[:, j % 2, 0],
                                              start=False, stop=last and j == 3)
                        if last and j == 3 and c < KC - 1:
                            mm.then_inc(v_done, 1)
                    mm.then_inc(gemm_done, 1)

            sum_panels(0, first=True)
            settle(pe)
            with pe.Fori(1, P // 4 - 1) as i:
                sum_panels(i * 4)
            sum_panels(P - 4, last=True)
        pe.wait_ge(x_added, DEPTH * KC + 3)
        for q in range(KC):
            sum_squares(pe, DEPTH, q, 2, q == 0, q == KC - 1)

    @block.scalar
    def _(act):
        act.wait_ge(c_in, 16)
        nc.scalar.activation(c_sig[:], c_act[:], ACT.Sigmoid).then_inc(c_ready, 1)
        act.wait_ge(rope_made, 1)
        nc.scalar.activation(sin[:], ang[:], ACT.Sin)
        nc.scalar.activation(cos[:], over[:], ACT.Sin).then_inc(rope_made, 1)

        def norm_h(l, which):
            if not which:
                for q in range(KC):
                    act.wait_ge(x_added, l * KC + q + 1)
                    square(act, l, SQ_H1 + q, x_sb[:, q])
            take_root(act, l, 3 * which, D)
            if not which:
                for m in range(LEAD):
                    split_hi(act, l, m)
            sh = (0, 3 * KC)[which]
            for c in range(KC):
                act.wait_ge(t_ready, l * 2 * KC + which * KC + c + 1)
                nc.scalar.activation(mov[:, 0, c], ht[:, c % 2], ACT.Identity, bias=mod[:, sh + c:sh + c + 1]
                                     ).then_inc(t_hi, 1)

        with act.Fori(0, DEPTH) as l:
            act.wait_ge(consts_made, 2)
            norm_h(l, 0)
            for kind, i in STEPS:
                if kind == "panel":
                    split_hi(act, l, i + LEAD)
                    bank = ps[:, i % 2]
                    act.wait_ge(gemm_done, 1 + l * M_ALL + i + 1)
                    if i < P_KR:
                        square(act, l, SQ_LAT + i, bank)
                        nc.scalar.copy(lat[:, i], bank).then_inc(bank_free[i % 2], 1)
                    elif i in FLIPPED:
                        f = FLIPPED.index(i)
                        if f >= 2:
                            act.wait_ge(flipped, l * N_FLIP + f - 1)
                        if P_ZV <= i < P_ZU:
                            ins = nc.scalar.activation(ytmp[:, f % 2], bank, ACT.Gelu_apprx_tanh)
                        else:
                            ins = nc.scalar.copy(ytmp[:, f % 2], bank)
                        ins.then_inc(bank_free[i % 2], 1)
                    elif i < P_ZP:
                        nc.scalar.activation(ug[:, i - P_ZU], bank, ACT.Gelu_apprx_tanh
                                             ).then_inc(bank_free[i % 2], 1)
                    else:
                        j = i - P_GATE
                        if j == 0:
                            act.wait_ge(proj_ready, l * 2 * TT + TT)
                        if j >= 6:
                            act.wait_ge(gate_out[j % 6], l * 64 + 16 * (j // 6))
                        nc.scalar.activation(gst[:, j % 6], bank, ACT.Tanh, scale=0.5).then_inc(bank_free[i % 2], 1)
                elif kind == "flip":
                    act.wait_ge(flipped, l * N_FLIP + i + 1)
                    tiles = ps[:, 7].rearrange("p (t c) -> p t c", t=TT)
                    if i == 0:
                        ins = nc.scalar.copy(kr[:], tiles[:, :, :ROPE])
                    else:
                        dst, j = ((vg, i - 1), (zp, i - 3))[i > 2]
                        ins = nc.scalar.copy(dst[:, :, j * P:(j + 1) * P], tiles)
                    ins.then_inc(flip_used, 1)
                elif kind == "root":
                    take_root(act, l, 1 + i, (Q_LORA, KV_LORA)[i])
                elif kind == "proj":
                    act.wait_ge(proj_ready, l * 2 * TT + i + 1)
                    if i >= 2:
                        act.wait_ge(turn_ready, l * 2 * TT + i - 1)
                    flat = ps[:, 4:6].rearrange("p b n -> p (b n)")
                    if i < TT:
                        nc.scalar.copy(tok[:, i % 2, :, :NOPE],
                                       flat[:, :HEADS * QK].rearrange("p (h c) -> p h c", c=QK)[:, :, :NOPE]
                                       ).then_inc(tok_act, 1)
                    else:
                        kv = flat.rearrange("p (h c) -> p h c", c=NOPE + VD)
                        nc.scalar.copy(tok[:, i % 2, :, :NOPE], kv[:, :, :NOPE])
                        nc.scalar.copy(vh[:, i - TT].rearrange("p (h c) -> p h c", c=VD), kv[:, :, NOPE:]
                                       ).then_inc(tok_act, 1)
                elif kind == "turn":
                    act.wait_ge(turn_ready, l * 2 * TT + i + 1)
                    dst, t = (qT if i < TT else kT), i % TT
                    nc.scalar.copy(dst[:QK, 0:4, t * P:(t + 1) * P],
                                   ps[:QK, 2].rearrange("p (h t) -> p h t", h=4)).then_inc(turn_act, 1)
                elif kind == "ln":
                    act.wait_ge(ln_var, l + 1)
                    nc.scalar.activation(lnr[:], bn2[:, :, 1], ACT.Sqrt, bias=eps[:]).then_inc(ln_root, 1)
                elif kind == "pt":
                    n = (i % TT + 1) * P
                    act.wait_ge(pt_ready, 1 + l * 32 + i + 1)
                    if i >= 2:
                        act.wait_ge(pv_ready, l * 32 + i - 1)
                    nc.scalar.copy(prT[:, i % 2, :n], ps[:, 4 + i % 2, :n]).then_inc(prT_ready, 1)
                elif kind == "y":
                    k = Y_ORDER[i]
                    if i == 0:
                        act.wait_ge(gemm_done, 1 + l * M_ALL + N_IN)
                        act.wait_ge(side_out, 1 + l * 12 + 12)
                    if 2 <= k < 6:
                        act.wait_ge(y_ready, 1 + l * HEADS + 2 * (k - 1))
                    nc.scalar.copy(mov[:, 0, k], y[:, k]).then_inc(y_hi, 1)
                elif kind == "qk":
                    n = (i % TT + 1) * P
                    act.wait_ge(max_ready, l * 32 + i + 1)
                    act.wait_ge(pt_ready, 1 + l * 32 + max(i - 1, 0))
                    act.wait_ge(side_ready, l * 12 + 12)
                    nc.scalar.activation(pr[:, i % 2, :n], ps[:, 2 + i % 2, :n], ACT.Exp,
                                         bias=nmx[:, i % 2:i % 2 + 1], scale=SCALE,
                                         accum_out=rsum[:, i % 2:i % 2 + 1]).then_inc(exp_ready, 1)
            split_hi(act, l, M_ABC + LEAD)
            for i in range(KC):
                split_hi(act, l, M_ABC + i + 1 + LEAD)
                act.wait_ge(merged, l * KC + i + 1)
                if i == 0:
                    act.wait_ge(pv_ready, l * 32 + 32)
                nc.scalar.copy(mrg[:, 0, i], ytmp[:, i % 2]).then_inc(merged_hi, 1)
            for i in range(KC):
                if i:
                    split_hi(act, l, M_WO + i + LEAD)
                act.wait_ge(*banked(M_WO + i, l))
                square(act, l, SQ_H2 + i, x_sb[:, i])
            norm_h(l, 1)

            def post_u(a, more, m, more_m):
                act.wait_ge(gemm_done, 1 + l * M_ALL + more_m + m + 1)
                act.wait_ge(h_out[a % 2], 16 + l * (8 * P) + more * 8 + 16 * (a // 2))
                nc.scalar.activation(hst[:, a % 2], ps[:, m % 2], ACT.Gelu_apprx_tanh
                                     ).then_inc(bank_free[m % 2], 1)

            settle(act)
            with act.Fori(0, PH) as h:
                for j in range(2 + T_U):
                    m, more = M_T + j, h * (2 + T_U)
                    split_hi(act, l, m + LEAD, more)
                    if j < 2:
                        act.wait_ge(gemm_done, 1 + l * M_ALL + more + m + 1)
                        act.wait_ge(score_ready, 1 + l * 2 * PH + h * 2)
                        nc.scalar.copy(qh[:, j], ps[:, m % 2]).then_inc(bank_free[m % 2], 1)
                    else:
                        post_u(j - 2, h * T_U, m, more)

            def experts(first_m, first_a, times):
                settle(act)
                with act.Fori(0, times) as i:
                    for j in range(4):
                        split_hi(act, l, first_m + j + LEAD, i * 4)
                        post_u(first_a + j, i * 4, first_m + j, i * 4)

            act.wait_ge(g_sub, l + 1)
            nc.scalar.activation(topv[:], topv[:], ACT.Exp).then_inc(g_exp, 1)
            experts(M_R1, A_R1, REST // 4)
            act.wait_ge(sel_turned, l + 1)
            nc.scalar.copy(sel1T[:], ps[:, 2])
            nc.scalar.copy(sel2T[:], ps[:, 3]).then_inc(sel_act, 1)
            settle(act)
            with act.Fori(0, NTB // 2) as b:
                for half in range(2):
                    for j in range(BLK_U):
                        jj = half * BLK_U + j
                        split_hi(act, l, M_G + jj + LEAD, b * (2 * BLK_U))
                        post_u(A_G + jj, b * (2 * BLK_U), M_G + jj, b * (2 * BLK_U))
                        for s in range(2 * j, 2 * j + 2):
                            e = half * 8 + s
                            act.wait_ge(gmm_done, 1 + l * (8 * NTB) + b * 16 + e + 1)
                            bank = 4 + 2 * (e % 2)
                            nc.scalar.copy(low[:, e % 2], ps[:, bank:bank + 2].rearrange(
                                "p b (t h a) -> p (b t) h a", t=2, h=2)[:, :, 1]).then_inc(low_ready, 1)
            experts(M_R2, A_R2, REST // 4)
            settle(act)
            with act.Fori(0, P // 4 - 1) as i:
                for j in range(4):
                    split_hi(act, l, M_V + j + LEAD, i * 4)
            for j in range(RING - LEAD):
                split_hi(act, l, M_ALL - (RING - LEAD) + j)
        for q in range(KC):
            act.wait_ge(x_added, DEPTH * KC + q + 1)
            square(act, DEPTH, q, x_sb[:, q])
        take_root(act, DEPTH, 0, D)

    @block.vector
    def _(dve):
        chain = Chain(dve, dve_step, dve_chain)
        dve.wait_ge(c_ready, 1)
        nc.vector.tensor_tensor(c_act[:], c_act[:], c_sig[:], ALU.mult).then_inc(c_ready, 1)
        dve.wait_ge(c_ready, 2)

        def first_columns(start, stop):
            for i in range(start, stop):
                dve.wait_ge(mod0_in[i % 4], 16 * (i // 4 + 1))
                mod_column(mod[:, i:i + 1], mod0[:, i % 4], mod0_done)

        dve.wait_ge(start_in, 16 * N_START)
        setup = Chain(dve, setup_step, 0)
        setup.link(nc.vector.tensor_copy(pos_f[:], pos_i[:]))
        for t in range(TT):
            last = nc.vector.tensor_scalar(ang[:, t], frq[:], pos_f[:, t:t + 1], None, ALU.mult)
        setup.link(last)
        magic, tau = 12582912.0, 2 * np.pi
        parts = [6.28125, 0.0019340515136718750]
        parts.append(tau - sum(parts))
        setup.link(nc.vector.tensor_scalar(turns[:], ang[:], 1.0 / tau, magic, ALU.mult, ALU.add))
        setup.link(nc.vector.tensor_scalar(turns[:], turns[:], magic, None, ALU.subtract))
        for part in parts:
            setup.link(nc.vector.scalar_tensor_tensor(ang[:], turns[:], -part, ang[:], ALU.mult, ALU.add))
        below = float(np.nextafter(np.float32(np.pi), np.float32(0)))
        setup.link(nc.vector.tensor_scalar(over[:], ang[:], float(np.pi / 2), None, ALU.add))
        setup.link(nc.vector.tensor_scalar(turns[:], over[:], below, -tau, ALU.is_gt, ALU.mult))
        setup.link(nc.vector.tensor_tensor(over[:], over[:], turns[:], ALU.add))
        setup.link(nc.vector.tensor_scalar(over[:], over[:], below, -below, ALU.min, ALU.max))
        nc.vector.tensor_scalar(ang[:], ang[:], below, -below, ALU.min, ALU.max).then_inc(rope_made, 1)

        first_columns(0, MOD_FIRST)
        dve.wait_ge(mod0_done, MOD_FIRST)

        def norm_h(l, which):
            rstd(dve, l, 3 * which)
            dve.wait_ge(rstd_ready, l * 4 + 3 * which + 1)
            sh, sc = (0, 3 * KC)[which], (KC, 4 * KC)[which]
            for c in range(KC + 1):
                if c < KC:
                    if c >= 2:
                        dve.wait_ge(mov_ready, l * 3 * KC + (0, 2 * KC)[which] + c - 1)
                    nc.vector.scalar_tensor_tensor(ht[:, c % 2], x_sb[:, c], mod[:, sc + c:sc + c + 1], root[:],
                                                   ALU.mult, ALU.mult).then_inc(t_ready, 1)
                if c:
                    n = which * KC + c - 1
                    dve.wait_ge(t_hi, l * 2 * KC + n + 1)
                    nc.vector.scalar_tensor_tensor(mov[:, 1, c - 1], ht[:, (c - 1) % 2],
                                                   mod[:, sh + c - 1:sh + c], mov[:, 0, c - 1].bitcast(F32),
                                                   ALU.add, ALU.subtract).then_inc(mov_ready, 1)
                if not which and c in (1, KC):
                    split_lo(dve, l, c // KC)

        with dve.Fori(0, DEPTH) as l:
            chain.start(l)
            dve.wait_ge(bias_in, l * 16 + 16)
            chain.link(nc.vector.tensor_tensor(mod[:, :MOD_FIRST], mod[:, :MOD_FIRST], bmod[:, :MOD_FIRST], ALU.add))
            chain.link(nc.vector.tensor_scalar(mod[:, KC:2 * KC], mod[:, KC:2 * KC], 1.0, None, ALU.add))
            norm_h(l, 0)
            for kind, i in STEPS:
                if kind == "panel":
                    for a in (0, 1) if i == 0 else (i + 1,):
                        if a < N_MODX:
                            n = RAW_OF[("mod", MOD_FIRST + a)]
                            dve.wait_ge(raw_in[n % RAW], l * (16 * RAW_USES) + 16 * (n // RAW + 1))
                            mod_column(mod[:, MOD_FIRST + a:MOD_FIRST + a + 1],
                                       raw[:, n % RAW].rearrange("p k c -> p (k c)"), mod_done)
                    split_lo(dve, l, i + LEAD)
                    if i == N_MODX:
                        dve.wait_ge(mod_done, l * N_MODX + N_MODX)
                        chain.link(nc.vector.tensor_tensor(mod[:, MOD_FIRST:], mod[:, MOD_FIRST:],
                                                           bmod[:, MOD_FIRST:], ALU.add))
                        chain.link(nc.vector.tensor_scalar(mod[:, 4 * KC:5 * KC], mod[:, 4 * KC:5 * KC], 1.0, None,
                                                           ALU.add))
                        chain.link(nc.vector.tensor_scalar(mod[:, 2 * KC:3 * KC], mod[:, 2 * KC:3 * KC], 0.5, None,
                                                           ALU.mult))
                elif kind == "flip" and i == 2:
                    dve.wait_ge(flip_used, 1 + l * N_FLIP + 3)
                    settle(dve)
                    for t in range(TT):
                        last = nc.vector.bn_stats(bn6[:, t], vg[:, t])
                    chain.link(last)
                    settle(dve)
                    for t in range(TT):
                        last = nc.vector.bn_aggr(bn2[:, t], bn6[:, t])
                    last.then_inc(ln_var, 1)
                elif kind == "root":
                    if i == 0:
                        dve.wait_ge(params_in, l * (16 * N_PARAMS) + 16 * N_PARAMS)
                    rstd(dve, l, 1 + i)
                    dve.wait_ge(rstd_ready, l * 4 + 2 + i)
                    for k in ((0, 1, 2), (3, 4))[i]:
                        dve.wait_ge(*banked(k, l))
                        nc.vector.scalar_tensor_tensor(lat[:, k], lat[:, k], gain[:, k:k + 1], root[:],
                                                       ALU.mult, ALU.mult).then_inc(lat_norm, 1)
                elif kind == "proj":
                    t = i % TT
                    dve.wait_ge(proj_ready, l * 2 * TT + i + 1)
                    if i == 0:
                        dve.wait_ge(rope_made, 2)
                    if i < TT:
                        src = ps[:, 4:6].rearrange("p b n -> p (b n)")[:, :HEADS * QK].rearrange(
                            "p (h c) -> p h c", c=QK)[:, :, NOPE:]
                        n = HEADS
                        dve.wait_ge(tok_act, 1 + l * 2 * TT + i + 1)
                    else:
                        src, n = kr[:, t:t + 1], 1
                        if i == TT:
                            dve.wait_ge(flip_used, 1 + l * N_FLIP + 1)
                    x1, x2 = src[:, :, :HALF], src[:, :, HALF:]
                    cs = cos[:, t:t + 1].to_broadcast([P, n, HALF])
                    sn = sin[:, t:t + 1].to_broadcast([P, n, HALF])
                    nc.vector.tensor_tensor(rt[:, 0, :n], x1, cs, ALU.mult)
                    nc.vector.tensor_tensor(rt[:, 1, :n], x2, sn, ALU.mult)
                    nc.vector.tensor_tensor(rt[:, 2, :n], x2, cs, ALU.mult)
                    chain.link(nc.vector.tensor_tensor(rt[:, 3, :n], x1, sn, ALU.mult))
                    if i >= 2:
                        dve.wait_ge(turn_ready, l * 2 * TT + i - 1)
                    dst = tok[:, i % 2, :, NOPE:]
                    if i < TT:
                        nc.vector.tensor_tensor(dst[:, :, :HALF], rt[:, 0], rt[:, 1], ALU.subtract)
                        nc.vector.tensor_tensor(dst[:, :, HALF:], rt[:, 2], rt[:, 3], ALU.add).then_inc(tok_dve, 1)
                        dve.wait_ge(tok_dve, 1 + l * 2 * TT + i + 1)
                    else:
                        a, b, c, d = (rt[:, j, :1].to_broadcast([P, HEADS, HALF]) for j in range(4))
                        nc.vector.tensor_tensor(dst[:, :, :HALF], a, b, ALU.subtract)
                        nc.vector.tensor_tensor(dst[:, :, HALF:], c, d, ALU.add).then_inc(tok_dve, 1)
                        dve.wait_ge(tok_dve, 1 + l * 2 * TT + i + 1)
                elif kind == "turn":
                    dve.wait_ge(turn_ready, l * 2 * TT + i + 1)
                    dst, t = (qT if i < TT else kT), i % TT
                    nc.vector.tensor_copy(dst[:QK, 4:8, t * P:(t + 1) * P],
                                          ps[:QK, 3].rearrange("p (h t) -> p h t", h=4)).then_inc(turn_dve, 1)
                elif kind == "ln":
                    dve.wait_ge(ln_root, l + 1)
                    chain.link(nc.vector.reciprocal(lnr[:], lnr[:]))
                    for t in range(TT):
                        last = nc.vector.tensor_scalar(vg[:, t], vg[:, t], bn2[:, t, 0:1], lnr[:, t:t + 1],
                                                       ALU.subtract, ALU.mult)
                    last.then_inc(ln_ready, 1)
                elif kind == "ya":
                    dve.wait_ge(side_ready, l * 12 + i + 1)
                    if i == 0:
                        dve.wait_ge(mid_in, l * (16 * N_MID) + 16 * N_MID)
                        dve.wait_ge(bank_free[1], 1 + l * N_BANKED + (P_ZU + 1) // 2 + 1)
                        dve.wait_ge(bank_free[0], 1 + l * N_BANKED + P_ZU // 2 + 1)
                    r0 = 64 * (i % 2)
                    chain.link(nc.vector.tensor_tensor(
                        ytmp[r0:r0 + 64, i % 2].rearrange("p (n t) -> p n t", n=TT),
                        ps[r0:r0 + 64, 4 + i % 2].rearrange("p (n t) -> p n t", n=TT),
                        bsb[r0:r0 + 64, i:i + 1].to_broadcast([64, TT, P]), ALU.add))
                    nc.vector.tensor_tensor(y[r0:r0 + 64, i // 2], ytmp[r0:r0 + 64, i % 2], ug[r0:r0 + 64, i // 2],
                                            ALU.mult).then_inc(side_out, 1)
                elif kind == "win":
                    e = 4 + (i if i < 2 else i + 2)
                    r0 = 64 * (i % 2)
                    dve.wait_ge(side_ready, l * 12 + e + 1)
                    dve.wait_ge(side_out, 1 + l * 12 + e)
                    nc.vector.tensor_copy(ytmp[r0:r0 + 64, i % 2], ps[r0:r0 + 64, 4 + i % 2]).then_inc(side_out, 1)
                elif kind == "pool":
                    e = 6 + (i if i < 2 else i + 2)
                    r0 = 64 * (i % 2)
                    dve.wait_ge(side_ready, l * 12 + e + 1)
                    nc.vector.tensor_scalar(y[r0:r0 + 64, 6 + i // 2], ps[r0:r0 + 64, 4 + i % 2],
                                            pscale[r0:r0 + 64, i // 2:i // 2 + 1], None, ALU.mult
                                            ).then_inc(side_out, 1)
                elif kind == "qk":
                    n, b = (i % TT + 1) * P, i % 2
                    dve.wait_ge(qk_ready, l * 32 + i + 1)
                    chain.link(nc.vector.tensor_reduce(mx[:, b:b + 1], ps[:, 2 + b, :n], AX, ALU.max))
                    nc.vector.tensor_scalar(nmx[:, b:b + 1], mx[:, b:b + 1], -SCALE, None, ALU.mult
                                            ).then_inc(max_ready, 1)
                elif kind == "norm":
                    n, b = (i % TT + 1) * P, i % 2
                    dve.wait_ge(exp_ready, 1 + l * 32 + i + 1)
                    chain.link(nc.vector.reciprocal(rinv[:, b:b + 1], rsum[:, b:b + 1]))
                    nc.vector.tensor_scalar(pr[:, b, :n], pr[:, b, :n], rinv[:, b:b + 1], None, ALU.mult
                                            ).then_inc(prob_ready, 1)
                elif kind == "y":
                    k = Y_ORDER[i]
                    dve.wait_ge(y_hi, l * KC + i + 1)
                    nc.vector.tensor_tensor(mov[:, 1, k], y[:, k], mov[:, 0, k].bitcast(F32), ALU.subtract
                                            ).then_inc(mov_ready, 1)
                elif kind == "pv" and i % TT == TT - 1:
                    h = i // TT
                    r0 = 64 * (h % 2)
                    dve.wait_ge(pv_ready, l * 32 + i + 1)
                    nc.vector.tensor_copy(y[r0:r0 + 64, 2 + h // 2], ps[r0:r0 + 64, 6]).then_inc(y_ready, 1)

            def merged_low(i):
                dve.wait_ge(merged_hi, l * KC + i + 1)
                nc.vector.tensor_tensor(mrg[:, 1, i], ytmp[:, i % 2], mrg[:, 0, i].bitcast(F32), ALU.subtract
                                        ).then_inc(merged_lo, 1)

            for i in range(KC):
                m = M_ABC + i
                split_lo(dve, l, m + LEAD)
                dve.wait_ge(gemm_done, 1 + l * M_ALL + m + 1)
                for b in range(3):
                    j = 3 * i + b
                    dve.wait_ge(gate_in[j % 6], l * 64 + 16 * (j // 6 + 1))
                if i >= 2:
                    dve.wait_ge(merged_lo, l * KC + i - 1)
                g = [gst[:, (3 * i + b) % 6] for b in range(3)]
                for b in range(3):
                    last = nc.vector.scalar_tensor_tensor(
                        g[b], g[b], 1.0, ps[:, (m % 2, 2 + m % 2, 4 + m % 2)[b]], ALU.add, ALU.mult)
                last.then_inc(bank_free[m % 2], 1)
                dve.wait_ge(bank_free[m % 2], 1 + l * N_BANKED + m // 2 + 1)
                if i:
                    merged_low(i - 1)
                chain.link(nc.vector.tensor_tensor(ytmp[:, i % 2], g[0], g[1], ALU.add))
                nc.vector.tensor_tensor(ytmp[:, i % 2], ytmp[:, i % 2], g[2], ALU.add).then_inc(merged, 1)
            merged_low(KC - 1)
            for i in range(KC):
                m = M_WO + i
                split_lo(dve, l, m + LEAD)
                dve.wait_ge(gemm_done, 1 + l * M_ALL + m + 1)
                nc.vector.scalar_tensor_tensor(x_sb[:, i], ps[:, m % 2], mod[:, 2 * KC + i:2 * KC + i + 1],
                                               x_sb[:, i], ALU.mult, ALU.add).then_inc(bank_free[m % 2], 1)
            norm_h(l, 1)

            settle(dve)
            with dve.Fori(0, PH) as h:
                more = h * (2 + T_U)
                chain.enter(h, 21)

                def best(side):
                    dve.wait_ge(score_ready, 1 + l * 2 * PH + h * 2 + side + 1)
                    sc = ps[:, 2 + side].rearrange("p (t k) -> p t k", t=TT)
                    settle(dve)
                    for t in range(TT):
                        last = nc.vector.max(v12[:, t, side, :8], sc[:, t])
                    chain.link(last)
                    settle(dve)
                    for t in range(TT):
                        nc.vector.max_index(i12u[:, t, side, :8], v12[:, t, side, :8], sc[:, t])
                        last = nc.vector.match_replace(sc2[:, t], v12[:, t, side, :8], sc[:, t], NEG)
                    last.then_inc(score_used, 1)
                    dve.wait_ge(score_used, 1 + l * 2 * PH + h * 2 + side + 1)
                    settle(dve)
                    for t in range(TT):
                        last = nc.vector.max(v12[:, t, side, 8:], sc2[:, t])
                    chain.link(last)
                    settle(dve)
                    for t in range(TT):
                        last = nc.vector.max_index(i12u[:, t, side, 8:], v12[:, t, side, 8:], sc2[:, t])
                    chain.link(last)
                    chain.link(nc.vector.tensor_copy(i12[:, :, side], i12u[:, :, side]))

                def pairs():
                    c4 = cand[:].rearrange("p t (a b) -> p t a b", a=TOPK)
                    chain.link(nc.vector.tensor_tensor(
                        c4, v12[:, :, 0].unsqueeze(3).to_broadcast([P, TT, TOPK, TOPK]),
                        v12[:, :, 1].unsqueeze(2).to_broadcast([P, TT, TOPK, TOPK]), ALU.add))
                    settle(dve)
                    for t in range(TT):
                        last = nc.vector.max(topc[:, t, :8], cand[:, t])
                    chain.link(last)
                    settle(dve)
                    for t in range(TT):
                        nc.vector.max_index(posu[:, t, :8], topc[:, t, :8], cand[:, t])
                        last = nc.vector.match_replace(cand2[:, t], topc[:, t, :8], cand[:, t], NEG)
                    chain.link(last)

                def pairs2():
                    settle(dve)
                    for t in range(TT):
                        last = nc.vector.max(topc[:, t, 8:], cand2[:, t])
                    chain.link(last)
                    settle(dve)
                    for t in range(TT):
                        last = nc.vector.max_index(posu[:, t, 8:], topc[:, t, 8:], cand2[:, t])
                    chain.link(last)
                    nc.vector.tensor_copy(topv[:, :, ds(h, 1)].rearrange("p t o k -> p t (o k)"), topc[:])
                    nc.vector.tensor_single_scalar(abu[:, 0], posu[:], 4, ALU.logical_shift_right)
                    chain.link(nc.vector.tensor_single_scalar(abu[:, 1], posu[:], 15, ALU.bitwise_and))
                    chain.link(nc.vector.tensor_copy(abf[:], abu[:]))

                def key_of(side):
                    e3 = eq[:].rearrange("p t k r -> p (t k) r")
                    chain.link(nc.vector.tensor_tensor(
                        e3, abf[:, side].rearrange("p t k -> p (t k)").unsqueeze(2).to_broadcast([P, TT * TOPK, TOPK]),
                        iota[:, :TOPK].unsqueeze(1).to_broadcast([P, TT * TOPK, TOPK]), ALU.is_equal))
                    chain.link(nc.vector.tensor_tensor(
                        eq[:], eq[:], i12[:, :, side].unsqueeze(2).to_broadcast([P, TT, TOPK, TOPK]), ALU.mult))
                    chain.link(nc.vector.tensor_reduce(
                        (sel1, sel2)[side][:, :, ds(h, 1)].rearrange("p t o k -> p t (o k)"), eq[:], AX, ALU.add))

                work = {2: lambda: best(0), 3: lambda: best(1), 4: pairs, 5: pairs2,
                        6: lambda: key_of(0), 7: lambda: key_of(1)}
                for j in range(2 + T_U):
                    split_lo(dve, l, M_T + j + LEAD, more)
                    if j in work:
                        work[j]()
            chain.leave(PH)

            t3 = topv[:].rearrange("p t h k -> p (t h) k")
            chain.link(nc.vector.tensor_copy(den[:], t3[:, :, 0]))
            nc.vector.tensor_tensor(t3, t3, den[:].unsqueeze(2).to_broadcast([P, TT * PH, TOPK]), ALU.subtract
                                    ).then_inc(g_sub, 1)

            def experts(first_m, times):
                settle(dve)
                with dve.Fori(0, times) as i:
                    for j in range(4):
                        split_lo(dve, l, first_m + j + LEAD, i * 4)

            dve.wait_ge(g_exp, l + 1)
            chain.link(nc.vector.tensor_reduce(den[:], t3, AX, ALU.add))
            chain.link(nc.vector.reciprocal(dinv[:], den[:]))
            nc.vector.tensor_tensor(t3, t3, dinv[:].unsqueeze(2).to_broadcast([P, TT * PH, TOPK]), ALU.mult
                                    ).then_inc(g_norm, 1)
            experts(M_R1, REST // 4)
            dve.wait_ge(sel_turned, l + 1)
            chain.link(nc.vector.tensor_copy(gT[:], ps[:, 4]))
            chain.link(nc.vector.tensor_copy(gThl[:, 0], gT[:]))
            nc.vector.tensor_tensor(gThl[:, 1], gT[:], gThl[:, 0].bitcast(F32), ALU.subtract).then_inc(sel_dve, 1)
            dve.wait_ge(sel_dve, l + 1)
            dve.wait_ge(sel_act, l + 1)
            settle(dve)
            with dve.Fori(0, NTB // 2) as b:
                for half in range(2):
                    for j in range(BLK_U):
                        jj = half * BLK_U + j
                        for s in range(2 * j, 2 * j + 2):
                            e = half * 8 + s
                            at = ds(b * (2 * TB) + (half * TB + 4 * s), 4)
                            four = lambda x: x.unsqueeze(2).to_broadcast([P, 4, P])
                            io = iota[:].unsqueeze(1).to_broadcast([P, 4, P])
                            nc.vector.tensor_tensor(hot1[:, e % 2], four(sel1T[:, at]), io, ALU.is_equal
                                                    ).then_inc(hot1_ready, 1)
                            nc.vector.tensor_tensor(hot2[:, e % 2], four(sel2T[:, at]), io, ALU.is_equal)
                            dve.wait_ge(hot1_ready, l * (8 * NTB) + b * 16 + e + 1)
                            nc.vector.tensor_tensor(hotg[:, e % 2, 0], hot1[:, e % 2],
                                                    four(gThl[:, 0, at].bitcast(F32)), ALU.mult).then_inc(hot_ready, 1)
                        split_lo(dve, l, M_G + jj + LEAD, b * (2 * BLK_U))
                        for s in range(2 * j, 2 * j + 2):
                            e = half * 8 + s
                            dve.wait_ge(low_ready, l * (8 * NTB) + b * 16 + e + 1)
                            if s == 0:
                                dve.wait_ge(stage_out[half], 16 + l * (8 * NTB) + b * 16)
                            bank = 4 + 2 * (e % 2)
                            parts = ps[:, bank:bank + 2].rearrange("p b (t h a) -> p (b t) h a", t=2, h=2)
                            nc.vector.tensor_tensor(stage[:, half, :, 4 * s:4 * s + 4].rearrange("p a t -> p t a"),
                                                    parts[:, :, 0], low[:, e % 2], ALU.add).then_inc(stage_ready, 1)
            experts(M_R2, REST // 4)
            def sum_panels(i, last=False):
                for j in range(8):
                    dve.wait_ge(gt_in[j // 4], l * (2 * P) + i * 16 + 16)
                    dve.wait_ge(hin_in[j % 4], l * (4 * P) + i * 32 + 16 * (j // 4 + 1))
                    chain.link(nc.vector.tensor_tensor(
                        wgt[:, j % 2].rearrange("p (b t) -> p b t", t=TB),
                        hin[:, j % 4].rearrange("p (b t) -> p b t", t=TB), gt[:, j // 4, :, j % 4], ALU.mult))
                    dve.wait_ge(gemm_done, 1 + l * M_ALL + i * 8 + (M_V + j - 1))
                    chain.link(nc.vector.tensor_copy(wgthl[:, j % 2, 0], wgt[:, j % 2]))
                    nc.vector.tensor_tensor(wgthl[:, j % 2, 1], wgt[:, j % 2], wgthl[:, j % 2, 0].bitcast(F32),
                                            ALU.subtract).then_inc(w_ready, 1)
                    if not last or j < 8 - LEAD:
                        split_lo(dve, l, M_V + j + LEAD, i * 8)
                    if j == 4:
                        dve.wait_ge(modv_in, l * (16 * MOD_FIRST) + i * 16 + 16)
                        settle(dve)
                        mod_column(mcol[:], modv[:], modv_done)
                        dve.wait_ge(modv_done, l * MOD_FIRST + i + 1)
                        chain.link(nc.vector.tensor_copy(mod[:, ds(i, 1)], mcol[:]))

            settle(dve)
            with dve.Fori(0, P // 8 - 1) as i:
                chain.enter(i, 17)
                sum_panels(i)
            chain.leave(P // 8 - 1)
            sum_panels(P // 8 - 1, last=True)
            for c in range(KC):
                if c < KC - 1:
                    dve.wait_ge(v_done, l * (KC - 1) + c + 1)
                else:
                    dve.wait_ge(gemm_done, 1 + l * M_ALL + M_ALL)
                nc.vector.scalar_tensor_tensor(x_sb[:, c], ps[:, c], mod[:, 5 * KC + c:5 * KC + c + 1], x_sb[:, c],
                                               ALU.mult, ALU.add).then_inc(x_added, 1)
            if dve_chain:
                assert chain.n == dve_chain, chain.n
            else:
                print("dve chain", chain.n)
        rstd(dve, DEPTH, 0)
        dve.wait_ge(rstd_ready, DEPTH * 4 + 1)
        for c in range(KC):
            nc.vector.scalar_tensor_tensor(x_sb[:, c], x_sb[:, c], fin[:, c:c + 1], root[:], ALU.mult, ALU.mult
                                           ).then_inc(out_ready, 1)

    block.__exit__(None, None, None)


def _constants():
    freq = (1.0 / (10000.0 ** (np.arange(0, ROPE, 2, dtype=np.float32) / ROPE))).astype(np.float32)
    s, t = np.arange(P)[:, None], np.arange(P)[None, :]
    band = np.zeros((P, 12, P), np.float32)
    for g, w in enumerate(WINDOWS):
        near = (s <= t) & (s > t - w)
        band[:, g] = near / np.float32(w) - (s == t)
        band[:, 4 + g] = (s > t + P - w) / np.float32(w)
        band[:, 8 + g] = near / np.minimum(t + 1, w).astype(np.float32) - (s == t)
    return np.ascontiguousarray(np.broadcast_to(freq, (P, HALF))), band


def _panels(w):
    l, r, c = w.shape
    return np.ascontiguousarray(w.reshape(l, r // P, P, c // P, P).transpose(0, 3, 2, 1, 4)).reshape(l * (c // P), P, r)


def _columns(v):
    return np.ascontiguousarray(np.swapaxes(v.reshape(v.shape[:-1] + (v.shape[-1] // P, P)), -1, -2))


def _rows(w):
    l, r, c = w.shape
    return np.ascontiguousarray(w.reshape(l, r // P, P, c).transpose(0, 2, 1, 3)).reshape(l, P, -1)


def kernel(**inputs):
    from concourse import bacc
    from concourse.bass_utils import run_bass_kernel_spmd

    a = {k: np.asarray(v) for k, v in inputs.items()}
    L = DEPTH
    freq, band = _constants()
    w = a["w_in"]
    at = np.cumsum([0, 256, 256, Q_LORA, KV_LORA, ROPE, 256, 3 * D])
    zu, zv, cq, ckv, kr, zp, zg = (w[:, :, at[i]:at[i + 1]] for i in range(7))
    zg = zg.reshape(L, D, 3, KC, P).transpose(0, 1, 3, 2, 4).reshape(L, D, 3 * D)
    w_in = np.concatenate([cq, ckv, kr, np.zeros((L, D, P - ROPE), w.dtype), zv, zu, zp, zg], axis=2)
    host = {
        "xT": np.ascontiguousarray(a["x"][0].T.reshape(KC, P, S).transpose(1, 0, 2)),
        "c": a["c"],
        "pos": np.ascontiguousarray(a["positions"][0].reshape(TT, P).T),
        "freq": freq,
        "bands": band,
        "w_mod": np.concatenate([a["w_mod"].transpose(0, 2, 1).reshape(L * N_MOD, P, D),
                                 np.zeros((MOD_FIRST, P, D), w.dtype)]),
        "b_mod": _columns(a["b_mod"]),
        "w_in": _panels(w_in),
        "w_sT": np.ascontiguousarray(a["w_s"].transpose(0, 3, 1, 2)).reshape(L, P, -1),
        "b_s": a["b_s"].reshape(L, -1),
        "qkv_gain": np.concatenate([_columns(a["q_norm"]), _columns(a["kv_norm"])], axis=2),
        "w_uq": _rows(a["w_uq"]),
        "w_ukv": _rows(a["w_ukv"]),
        "w_pool": np.ascontiguousarray(a["w_pool"].reshape(L, 2, 2, 64, 64).transpose(0, 2, 3, 1, 4)).reshape(L, P, -1),
        "pool_scale": _columns(a["pool_scale"]),
        "w_abc": _panels(np.concatenate([a["w_a"], a["w_b"], a["w_c"]], axis=1)),
        "w_o": _panels(a["w_o"]),
        "w_pq": _panels(a["w_pq"]),
        "keysT": np.ascontiguousarray(a["sub_keys"].transpose(0, 4, 1, 2, 3)).reshape(L, P, -1),
        "uT_tab": np.ascontiguousarray(a["u_tab"].reshape(L, P, P, KC, P).transpose(0, 1, 4, 3, 2)).reshape(L * P, P, D),
        "v_tab": a["v_tab"].reshape(L * P, P, D),
        "fin_gain": _columns(a["final_norm"]),
    }
    nc = bacc.Bacc("TRN2", target_bir_lowering=False, num_devices=1)
    args = {k: nc.dram_tensor(f"in_{k}", v.shape, mybir.dt.from_np(v.dtype), kind="ExternalInput").ap()
            for k, v in host.items()}
    args["out"] = nc.dram_tensor("out_x", (P, KC, S), F32, kind="ExternalOutput").ap()
    build_trunk(nc, dve_chain=DVE_CHAIN, **args)
    r = run_bass_kernel_spmd(nc, [{f"in_{k}": v for k, v in host.items()}], core_ids=[0])
    got = r.results[0]["out_x"]
    return np.ascontiguousarray(got.transpose(1, 0, 2).reshape(D, S).T)[None]
```
